# Optimizing a Trainium2 kernel written in Bass

```python
import jax, jax.numpy as jnp
from jax import lax
import numpy as np
import math

D_MODEL = 1024
BATCH = 1
SEQ = 256
DEPTH = 2

N_BRANCH = 4
HEAD_DIM = 64
BRANCH_WIDTH = D_MODEL // N_BRANCH
N_HEADS = BRANCH_WIDTH // HEAD_DIM
NORM_EPS = 1e-6
RW_DECAY_LORA = 64
RW_AAA_LORA = 64
RW_GATE_LORA = 128
RW_DECAY_SCALE = 0.606531
RW_LN_EPS = 64e-5
SB_BLOCK = 128
RET_CHUNK = 128
RET_GN_EPS = 1e-5
ROPE_BASE = 10000.0
CONV_WIDTH = 31
CONV_LN_EPS = 1e-5
D_FF = 2816
N_EXPERTS = 8
TOP_K = 2
D_FF_EXPERT = 1408
MOE_BLOCK = 256

RW_IN = 3 * BRANCH_WIDTH + RW_DECAY_LORA + RW_AAA_LORA + RW_GATE_LORA
SB_IN = 3 * BRANCH_WIDTH
RET_IN = 4 * BRANCH_WIDTH
CONV_IN = 2 * BRANCH_WIDTH
N_IN = RW_IN + SB_IN + RET_IN + CONV_IN
MIX_SPLITS = [RW_IN, RW_IN + SB_IN, RW_IN + SB_IN + RET_IN]
RW_SPLITS = [BRANCH_WIDTH, 2 * BRANCH_WIDTH, 3 * BRANCH_WIDTH,
             3 * BRANCH_WIDTH + RW_DECAY_LORA, 3 * BRANCH_WIDTH + RW_DECAY_LORA + RW_AAA_LORA]


def _rmsnorm(x, gain, eps=NORM_EPS):
    x32 = x.astype(jnp.float32)
    y = x32 * lax.rsqrt(jnp.mean(x32 * x32, axis=-1, keepdims=True) + eps)
    return (y * gain).astype(x.dtype)

def _layernorm(x, gain, bias, eps):
    x32 = x.astype(jnp.float32)
    xc = x32 - jnp.mean(x32, axis=-1, keepdims=True)
    var = jnp.mean(xc * xc, axis=-1, keepdims=True)
    return (xc * lax.rsqrt(var + eps) * gain + bias).astype(x.dtype)

def _token_shift(x):
    return jnp.pad(x, ((0, 0), (1, 0), (0, 0)))[:, :-1]

def _split_heads(t):
    return t.reshape(t.shape[0], t.shape[1], N_HEADS, HEAD_DIM)

def _rwkv7_mixer(p, mu, w0, w2, a0, a2, g2, k_k, k_a, r_k, ln_w, ln_b):
    B, S, _ = p.shape
    p = p + (_token_shift(p) - p) * mu
    r, k, v, pw, pa, pg = jnp.split(p, RW_SPLITS, axis=-1)
    w = jnp.exp(-RW_DECAY_SCALE * jax.nn.sigmoid((w0 + jnp.tanh(pw) @ w2).astype(jnp.float32)))
    a = jax.nn.sigmoid(a0 + pa @ a2)
    g = jax.nn.sigmoid(pg) @ g2
    r, k, v, w, a = (_split_heads(t) for t in (r, k, v, w, a))
    kk32 = (k * k_k.reshape(N_HEADS, HEAD_DIM)).astype(jnp.float32)
    kk = kk32 / jnp.maximum(jnp.sqrt(jnp.sum(kk32 * kk32, axis=-1, keepdims=True)), 1e-12)
    k = k * (1.0 + (a - 1.0) * k_a.reshape(N_HEADS, HEAD_DIM))

    def step(state, inp):
        r_t, w_t, k_t, v_t, kk_t, a_t = inp
        sa = jnp.einsum('bhvk,bhk->bhv', state, -kk_t)
        state = (state * w_t[:, :, None, :] + sa[..., None] * (kk_t * a_t)[:, :, None, :]
                 + v_t[..., None] * k_t[:, :, None, :])
        return state, jnp.einsum('bhvk,bhk->bhv', state, r_t)

    seq_first = lambda t: jnp.moveaxis(t.astype(jnp.float32), 1, 0)
    state0 = jnp.zeros((B, N_HEADS, HEAD_DIM, HEAD_DIM), jnp.float32)
    _, y = lax.scan(step, state0, tuple(seq_first(t) for t in (r, w, k, v, kk, a)))
    y = jnp.moveaxis(y, 0, 1)
    y = _layernorm(y, ln_w.reshape(N_HEADS, HEAD_DIM), ln_b.reshape(N_HEADS, HEAD_DIM), RW_LN_EPS)
    y = y + jnp.sum(r * k * r_k, axis=-1, keepdims=True) * v
    return (y.reshape(B, S, BRANCH_WIDTH) * g).astype(p.dtype)

def _stick_breaking_mixer(p, q_norm, k_norm):
    B, S, _ = p.shape
    nb = S // SB_BLOCK
    blocks = lambda t: _split_heads(t).reshape(B, nb, SB_BLOCK, N_HEADS, HEAD_DIM).transpose(0, 3, 1, 2, 4)
    q, k, v = (blocks(t) for t in jnp.split(p, 3, axis=-1))
    q = _rmsnorm(q, q_norm) * (HEAD_DIM ** -0.5)
    k = _rmsnorm(k, k_norm)
    idx = jnp.arange(SB_BLOCK)
    rev_incl = (idx[:, None] >= idx[None, :]).astype(jnp.float32)
    diag_mask = idx[None, :] < idx[:, None]
    acc = jnp.zeros((B, N_HEADS, nb, SB_BLOCK), jnp.float32)
    o = jnp.zeros((B, N_HEADS, nb, SB_BLOCK, HEAD_DIM), jnp.float32)
    for d in range(nb):
        n = nb - d
        z = jnp.einsum('bhnqd,bhnkd->bhnqk', q[:, :, d:], k[:, :, :n]).astype(jnp.float32)
        ls = jax.nn.log_sigmoid(-z)
        if d == 0:
            ls = jnp.where(diag_mask, ls, 0.0)
        cum = jnp.einsum('bhnqk,kj->bhnqj', ls, rev_incl)
        log_a = z + cum + acc[:, :, d:, :, None]
        if d == 0:
            log_a = jnp.where(diag_mask, log_a, -jnp.inf)
        attn = jnp.exp(log_a)
        o = o.at[:, :, d:].add(jnp.einsum('bhnqk,bhnkd->bhnqd', attn.astype(v.dtype), v[:, :, :n]).astype(jnp.float32))
        acc = acc.at[:, :, d:].add(cum[..., 0])
    return o.transpose(0, 2, 3, 1, 4).reshape(B, S, BRANCH_WIDTH).astype(p.dtype)

def _rotary(t):
    S = t.shape[1]
    inv_freq = ROPE_BASE ** (-jnp.arange(0, HEAD_DIM, 2, dtype=jnp.float32) / HEAD_DIM)
    ang = jnp.arange(S, dtype=jnp.float32)[:, None] * inv_freq[None, :]
    cos = jnp.cos(ang)[None, :, None, :].astype(t.dtype)
    sin = jnp.sin(ang)[None, :, None, :].astype(t.dtype)
    t1, t2 = jnp.split(t, 2, axis=-1)
    return jnp.concatenate([t1 * cos - t2 * sin, t1 * sin + t2 * cos], axis=-1)

def _retention_mixer(p, gn_w):
    B, S, _ = p.shape
    dt = p.dtype
    q, k, v, gt = jnp.split(p, 4, axis=-1)
    q = _rotary(_split_heads(q))
    k = _rotary(_split_heads(k)) * (HEAD_DIM ** -0.5)
    v = _split_heads(v)
    nc = S // RET_CHUNK
    chunk = lambda t: t.reshape(B, nc, RET_CHUNK, N_HEADS, HEAD_DIM).transpose(0, 3, 1, 2, 4)
    qc, kc, vc = chunk(q), chunk(k), chunk(v)
    log_gamma = jnp.log(1.0 - 2.0 ** (-5.0 - jnp.arange(N_HEADS, dtype=jnp.float32)))
    idx = jnp.arange(RET_CHUNK, dtype=jnp.float32)
    rel = idx[:, None] - idx[None, :]
    intra_decay = jnp.where(rel >= 0, jnp.exp(jnp.maximum(rel, 0.0) * log_gamma[:, None, None]), 0.0)
    k_decay = jnp.exp((RET_CHUNK - 1 - idx)[None, :] * log_gamma[:, None])
    q_decay = jnp.exp((idx + 1.0)[None, :] * log_gamma[:, None])
    chunk_decay = jnp.exp(RET_CHUNK * log_gamma)
    scores = jnp.einsum('bhcqd,bhckd->bhcqk', qc, kc) * intra_decay[None, :, None].astype(dt)
    intra = jnp.einsum('bhcqk,bhckd->bhcqd', scores, vc)
    kv = jnp.einsum('bhckd,bhcke->cbhde', kc * k_decay[None, :, None, :, None].astype(dt), vc)

    def step(state, kv_c):
        return chunk_decay[None, :, None, None] * state + kv_c, state

    _, state_prev = lax.scan(step, jnp.zeros(kv.shape[1:], jnp.float32), kv.astype(jnp.float32))
    inter = jnp.einsum('bhcqd,cbhde->bhcqe', qc * q_decay[None, :, None, :, None].astype(dt),
                       state_prev.astype(dt))
    o = (intra + inter).transpose(0, 2, 3, 1, 4).reshape(B, S, N_HEADS, HEAD_DIM)
    o = _layernorm(o, gn_w.reshape(N_HEADS, HEAD_DIM), 0.0, RET_GN_EPS)
    return o.reshape(B, S, BRANCH_WIDTH) * jax.nn.silu(gt)

def _conformer_conv_mixer(p, dw, db, ln_w, ln_b):
    u_a, u_b = jnp.split(p, 2, axis=-1)
    u = u_a * jax.nn.sigmoid(u_b)
    u = lax.conv_general_dilated(u, dw[:, None, :].astype(u.dtype), window_strides=(1,),
                                 padding=[(CONV_WIDTH - 1, 0)],
                                 dimension_numbers=('NWC', 'WIO', 'NWC'),
                                 feature_group_count=BRANCH_WIDTH) + db
    return jax.nn.silu(_layernorm(u, ln_w, ln_b, CONV_LN_EPS))

def _swiglu(h, w1, w3, w2):
    return (jax.nn.silu(h @ w1) * (h @ w3)) @ w2

def _moe_ffn(h, router, w1, w3, w2):
    B, S, D = h.shape
    T = B * S
    xt = h.reshape(T, D)
    logits = (xt @ router).astype(jnp.float32)
    top_logit, top_idx = lax.top_k(logits, TOP_K)
    gates = jax.nn.softmax(top_logit, axis=-1)
    n_assign = T * TOP_K
    expert = top_idx.reshape(-1)
    token = jnp.arange(n_assign) // TOP_K
    order = jnp.argsort(expert)
    expert_s, token_s, weight_s = expert[order], token[order], gates.reshape(-1)[order]
    x_s = xt[token_s]
    counts = jnp.bincount(expert, length=N_EXPERTS)
    n_blk = n_assign // MOE_BLOCK
    seg_start = jnp.sort(jnp.concatenate([jnp.arange(n_blk) * MOE_BLOCK, jnp.cumsum(counts)[:-1]]))
    seg_end = jnp.concatenate([seg_start[1:], jnp.array([n_assign], seg_start.dtype)])
    seg_blk = jnp.minimum(seg_start // MOE_BLOCK, n_blk - 1)
    seg_exp = expert_s[jnp.minimum(seg_start, n_assign - 1)]

    def segment(args):
        start, end, blk, e = args
        rows = blk * MOE_BLOCK + jnp.arange(MOE_BLOCK)
        xb = lax.dynamic_slice_in_dim(x_s, blk * MOE_BLOCK, MOE_BLOCK, axis=0)
        yb = _swiglu(xb, w1[e], w3[e], w2[e])
        return jnp.where(((rows >= start) & (rows < end))[:, None], yb, 0.0)

    y_seg = lax.map(segment, (seg_start, seg_end, seg_blk, seg_exp))
    y_s = jax.ops.segment_sum(y_seg, seg_blk, num_segments=n_blk).reshape(n_assign, D)
    out = jax.ops.segment_sum(y_s * weight_s[:, None].astype(y_s.dtype), token_s, num_segments=T)
    return out.reshape(B, S, D)

def first_inputs(seed: int = 0) -> dict:
    key = jax.random.key(seed)
    ks = iter(jax.random.split(key, 40))
    nrm = lambda shape, scale: scale * jax.random.normal(next(ks), shape, jnp.float32)
    L, C = DEPTH, BRANCH_WIDTH
    nd, nm = (DEPTH + 1) // 2, DEPTH // 2
    return {
        "x": nrm((BATCH, SEQ, D_MODEL), 1.0),
        "norm_mix": 1.0 + nrm((L, D_MODEL), 0.1),
        "w_in": nrm((L, D_MODEL, N_IN), D_MODEL ** -0.5),
        "rw_mu": jax.random.uniform(next(ks), (L, RW_IN), jnp.float32),
        "rw_w0": -1.5 + nrm((L, C), 0.5),
        "rw_w2": nrm((L, RW_DECAY_LORA, C), 0.5 * RW_DECAY_LORA ** -0.5),
        "rw_a0": nrm((L, C), 0.5),
        "rw_a2": nrm((L, RW_AAA_LORA, C), RW_AAA_LORA ** -0.5),
        "rw_g2": nrm((L, RW_GATE_LORA, C), RW_GATE_LORA ** -0.5),
        "rw_k_k": 0.85 + nrm((L, C), 0.1),
        "rw_k_a": 1.0 + nrm((L, C), 0.1),
        "rw_r_k": nrm((L, N_HEADS, HEAD_DIM), 0.1),
        "rw_ln_w": 1.0 + nrm((L, C), 0.1),
        "rw_ln_b": nrm((L, C), 0.01),
        "sb_q_norm": 1.0 + nrm((L, HEAD_DIM), 0.1),
        "sb_k_norm": 1.0 + nrm((L, HEAD_DIM), 0.1),
        "ret_gn": 1.0 + nrm((L, C), 0.1),
        "conv_dw": nrm((L, CONV_WIDTH, C), CONV_WIDTH ** -0.5),
        "conv_b": nrm((L, C), 0.01),
        "conv_ln_w": 1.0 + nrm((L, C), 0.1),
        "conv_ln_b": nrm((L, C), 0.01),
        "w_gate": nrm((L, N_BRANCH, D_MODEL, D_MODEL), D_MODEL ** -0.5),
        "w_branch": nrm((L, N_BRANCH, C, D_MODEL), C ** -0.5),
        "w_out": nrm((L, D_MODEL, D_MODEL), 0.5 * D_MODEL ** -0.5),
        "norm_ffn": 1.0 + nrm((L, D_MODEL), 0.1),
        "ffn_w1": nrm((nd, D_MODEL, D_FF), D_MODEL ** -0.5),
        "ffn_w3": nrm((nd, D_MODEL, D_FF), D_MODEL ** -0.5),
        "ffn_w2": nrm((nd, D_FF, D_MODEL), 0.5 * D_FF ** -0.5),
        "router": nrm((nm, D_MODEL, N_EXPERTS), D_MODEL ** -0.5),
        "moe_w1": nrm((nm, N_EXPERTS, D_MODEL, D_FF_EXPERT), D_MODEL ** -0.5),
        "moe_w3": nrm((nm, N_EXPERTS, D_MODEL, D_FF_EXPERT), D_MODEL ** -0.5),
        "moe_w2": nrm((nm, N_EXPERTS, D_FF_EXPERT, D_MODEL), 0.5 * D_FF_EXPERT ** -0.5),
    }

def first_block(x, norm_mix, w_in, rw_mu, rw_w0, rw_w2, rw_a0, rw_a2, rw_g2, rw_k_k, rw_k_a, rw_r_k,
              rw_ln_w, rw_ln_b, sb_q_norm, sb_k_norm, ret_gn, conv_dw, conv_b, conv_ln_w, conv_ln_b,
              w_gate, w_branch, w_out, norm_ffn, ffn_w1, ffn_w3, ffn_w2, router, moe_w1, moe_w3, moe_w2):
    for l in range(DEPTH):
        h = _rmsnorm(x, norm_mix[l])
        p_rw, p_sb, p_ret, p_conv = jnp.split(h @ w_in[l], MIX_SPLITS, axis=-1)
        branches = (
            _rwkv7_mixer(p_rw, rw_mu[l], rw_w0[l], rw_w2[l], rw_a0[l], rw_a2[l], rw_g2[l],
                         rw_k_k[l], rw_k_a[l], rw_r_k[l], rw_ln_w[l], rw_ln_b[l]),
            _stick_breaking_mixer(p_sb, sb_q_norm[l], sb_k_norm[l]),
            _retention_mixer(p_ret, ret_gn[l]),
            _conformer_conv_mixer(p_conv, conv_dw[l], conv_b[l], conv_ln_w[l], conv_ln_b[l]),
        )
        merged = jax.nn.sigmoid(h @ w_gate[l, 0]) * (branches[0] @ w_branch[l, 0])
        for i in range(1, N_BRANCH):
            merged = merged + jax.nn.sigmoid(h @ w_gate[l, i]) * (branches[i] @ w_branch[l, i])
        x = x + merged @ w_out[l]
        h = _rmsnorm(x, norm_ffn[l])
        if l % 2 == 0:
            x = x + _swiglu(h, ffn_w1[l // 2], ffn_w3[l // 2], ffn_w2[l // 2])
        else:
            x = x + _moe_ffn(h, router[l // 2], moe_w1[l // 2], moe_w3[l // 2], moe_w2[l // 2])
    return x


DEPTH_2 = 1

N_HEADS_2 = 8
N_KV_GROUPS = 2
GROUP_SIZE = N_HEADS_2 // N_KV_GROUPS
NSA_WIDTH = N_HEADS_2 * HEAD_DIM
KV_WIDTH = N_KV_GROUPS * HEAD_DIM
CMP_STRIDE = 16
CMP_BLOCK = 2 * CMP_STRIDE
CMP_HIDDEN = 256
SEL_BLOCK = 64
SEL_PER_CMP = SEL_BLOCK // CMP_STRIDE
N_SELECT = 16
WINDOW = 512
Q_BLOCK = 128
LRU_WIDTH = 512
LRU_BLOCKS = 8
LRU_BLOCK_DIM = LRU_WIDTH // LRU_BLOCKS
CONV_WIDTH_2 = 4
LRU_C = 8.0
N_BUCKETS = 32
MAX_DISTANCE = 128
N_BRANCHES = 2
EPS = 1e-6
NEG = -1e30
FORCE_SCORE = 1e9
IN_SIZES = (NSA_WIDTH, 6 * KV_WIDTH, NSA_WIDTH, 3 * N_HEADS_2, LRU_WIDTH, LRU_WIDTH, N_BRANCHES * D_MODEL)
D_IN = NSA_WIDTH + 6 * KV_WIDTH + NSA_WIDTH + 3 * N_HEADS_2 + LRU_WIDTH + LRU_WIDTH + N_BRANCHES * D_MODEL


def rms_norm(x, g):
    xf = x.astype(jnp.float32)
    y = xf * lax.rsqrt(jnp.mean(xf * xf, axis=-1, keepdims=True) + EPS)
    return (y * g.astype(jnp.float32)).astype(x.dtype)

def t5_bucket(dist):
    n = jnp.maximum(dist, 0)
    max_exact = N_BUCKETS // 2
    nf = jnp.maximum(n, 1).astype(jnp.float32)
    large = max_exact + (jnp.log(nf / max_exact) / math.log(MAX_DISTANCE / max_exact)
                         * (N_BUCKETS - max_exact)).astype(jnp.int32)
    large = jnp.minimum(large, N_BUCKETS - 1)
    return jnp.where(n < max_exact, n, large)

def masked_softmax(s, mask):
    s = jnp.where(mask, s.astype(jnp.float32), NEG)
    return jax.nn.softmax(s, axis=-1) * mask

def compress_blocks(kv, pe, w1, b1, w2):
    B, S, G, dh = kv.shape
    ch = kv.reshape(B, S // CMP_STRIDE, CMP_STRIDE, G, dh)
    blocks = jnp.concatenate([ch[:, :-1], ch[:, 1:]], axis=2)
    blocks = blocks + pe[None, None, :, None, :]
    nc = blocks.shape[1]
    flat = blocks.transpose(0, 1, 3, 2, 4).reshape(B, nc, G, CMP_BLOCK * dh)
    return jax.nn.silu(flat @ w1 + b1) @ w2

def second_inputs(seed: int = 0) -> dict:
    key = jax.random.key(seed)
    ks = jax.random.split(key, 24)
    nrm = lambda k, shape, s: jax.random.normal(k, shape, jnp.float32) * s
    u = jax.random.uniform(ks[17], (LRU_WIDTH,), jnp.float32, 0.9, 0.999)
    sig = u ** (1.0 / LRU_C)
    lru_lambda = jnp.log(sig) - jnp.log1p(-sig)
    return {
        "x": nrm(ks[0], (BATCH, SEQ, D_MODEL), 1.0),
        "norm_gain": 1.0 + nrm(ks[1], (D_MODEL,), 0.1),
        "w_in": nrm(ks[2], (D_MODEL, D_IN), D_MODEL ** -0.5),
        "q_norm_gain": 1.0 + nrm(ks[3], (HEAD_DIM,), 0.1),
        "k_norm_gain": 1.0 + nrm(ks[4], (3, HEAD_DIM), 0.1),
        "cmp_pe": nrm(ks[5], (2, CMP_BLOCK, HEAD_DIM), 0.5),
        "cmp_w1": nrm(ks[6], (2, CMP_BLOCK * HEAD_DIM, CMP_HIDDEN), (CMP_BLOCK * HEAD_DIM) ** -0.5),
        "cmp_b1": nrm(ks[7], (2, CMP_HIDDEN), 0.02),
        "cmp_w2": nrm(ks[8], (2, CMP_HIDDEN, HEAD_DIM), CMP_HIDDEN ** -0.5),
        "rel_bias": nrm(ks[9], (N_BUCKETS, N_HEADS_2), 0.5),
        "conv_w": nrm(ks[10], (CONV_WIDTH_2, LRU_WIDTH), CONV_WIDTH_2 ** -0.5),
        "conv_b": nrm(ks[11], (LRU_WIDTH,), 0.02),
        "lru_wa": nrm(ks[12], (LRU_BLOCKS, LRU_BLOCK_DIM, LRU_BLOCK_DIM), LRU_BLOCK_DIM ** -0.5),
        "lru_ba": nrm(ks[13], (LRU_WIDTH,), 0.02),
        "lru_wx": nrm(ks[14], (LRU_BLOCKS, LRU_BLOCK_DIM, LRU_BLOCK_DIM), LRU_BLOCK_DIM ** -0.5),
        "lru_bx": nrm(ks[15], (LRU_WIDTH,), 0.02),
        "lru_lambda": lru_lambda,
        "w_proj_a": nrm(ks[18], (NSA_WIDTH, D_MODEL), NSA_WIDTH ** -0.5),
        "w_proj_b": nrm(ks[19], (LRU_WIDTH, D_MODEL), LRU_WIDTH ** -0.5),
        "w_out": nrm(ks[20], (D_MODEL, D_MODEL), D_MODEL ** -0.5),
    }

def nsa_mixer(q, k_cmp, v_cmp, k_slc, v_slc, k_win, v_win, br_gate, q_norm_gain, k_norm_gain,
              cmp_pe, cmp_w1, cmp_b1, cmp_w2, rel_bias):
    B, S, _ = q.shape
    G, R, dh = N_KV_GROUPS, GROUP_SIZE, HEAD_DIM
    nsb = S // SEL_BLOCK
    n_sel = min(N_SELECT, nsb)
    scale = dh ** -0.5

    q = (rms_norm(q.reshape(B, S, G, R, dh), q_norm_gain) * scale).transpose(0, 2, 3, 1, 4)
    kc = rms_norm(compress_blocks(k_cmp, cmp_pe[0], cmp_w1[0], cmp_b1[0], cmp_w2[0]), k_norm_gain[0])
    vc = compress_blocks(v_cmp, cmp_pe[1], cmp_w1[1], cmp_b1[1], cmp_w2[1])
    kc = kc.transpose(0, 2, 1, 3)
    vc = vc.transpose(0, 2, 1, 3)
    nc = kc.shape[2]
    k_blocks = rms_norm(k_slc, k_norm_gain[1]).transpose(0, 2, 1, 3).reshape(B, G, nsb, SEL_BLOCK, dh)
    v_blocks = v_slc.transpose(0, 2, 1, 3).reshape(B, G, nsb, SEL_BLOCK, dh)
    pad_w = ((0, 0), (0, 0), (WINDOW, 0), (0, 0))
    k_wp = jnp.pad(rms_norm(k_win, k_norm_gain[2]).transpose(0, 2, 1, 3), pad_w)
    v_wp = jnp.pad(v_win.transpose(0, 2, 1, 3), pad_w)

    bias_gr = rel_bias.reshape(N_BUCKETS, G, R)
    def shared_bias(dist):
        return rel_bias[t5_bucket(dist)].transpose(2, 0, 1).reshape(G, R, *dist.shape)
    def group_bias(dist):
        b = jax.vmap(lambda tab, bk: tab[bk], in_axes=(1, 1), out_axes=1)(bias_gr, t5_bucket(dist))
        return jnp.moveaxis(b, -1, 2)

    c_end = jnp.arange(nc, dtype=jnp.int32) * CMP_STRIDE + CMP_BLOCK - 1
    blk = jnp.arange(nsb, dtype=jnp.int32)
    bi = jnp.arange(B)[:, None, None, None]
    gi = jnp.arange(G)[None, :, None, None]
    right_pad = SEL_PER_CMP * nsb + SEL_PER_CMP - 1 - nc

    def block_fn(q0):
        qc = lax.dynamic_slice_in_dim(q, q0, Q_BLOCK, axis=3)
        t = q0 + jnp.arange(Q_BLOCK, dtype=jnp.int32)
        dist = t[:, None] - c_end[None, :]
        s = jnp.einsum('bgrqd,bgcd->bgrqc', qc, kc) + shared_bias(dist)
        p_cmp = masked_softmax(s, dist >= 0)
        o_cmp = jnp.einsum('bgrqc,bgcd->bgrqd', p_cmp.astype(vc.dtype), vc)
        imp = jnp.pad(p_cmp.sum(axis=2), ((0, 0), (0, 0), (0, 0), (1, right_pad)))
        imp_blk = (imp[..., :SEL_PER_CMP * nsb].reshape(B, G, Q_BLOCK, nsb, SEL_PER_CMP).sum(-1)
                   + imp[..., SEL_PER_CMP:SEL_PER_CMP * nsb + SEL_PER_CMP:SEL_PER_CMP])
        cur = (t // SEL_BLOCK)[:, None]
        valid = blk[None, :] <= cur
        force = (blk[None, :] == 0) | (blk[None, :] == cur) | (blk[None, :] == cur - 1)
        score = jnp.where(valid, jnp.where(force, FORCE_SCORE, imp_blk), -1.0)
        _, idx = lax.top_k(score, n_sel)
        kb = k_blocks[bi, gi, idx].reshape(B, G, Q_BLOCK, n_sel * SEL_BLOCK, dh)
        vb = v_blocks[bi, gi, idx].reshape(B, G, Q_BLOCK, n_sel * SEL_BLOCK, dh)
        pos = (idx[..., None] * SEL_BLOCK + jnp.arange(SEL_BLOCK, dtype=jnp.int32)).reshape(B, G, Q_BLOCK, -1)
        dist = t[None, None, :, None] - pos
        s = jnp.einsum('bgrqd,bgqkd->bgrqk', qc, kb) + group_bias(dist)
        p = masked_softmax(s, (dist >= 0)[:, :, None])
        o_slc = jnp.einsum('bgrqk,bgqkd->bgrqd', p.astype(vb.dtype), vb)
        kw = lax.dynamic_slice_in_dim(k_wp, q0, WINDOW + Q_BLOCK, axis=2)
        vw = lax.dynamic_slice_in_dim(v_wp, q0, WINDOW + Q_BLOCK, axis=2)
        pos = q0 - WINDOW + jnp.arange(WINDOW + Q_BLOCK, dtype=jnp.int32)
        dist = t[:, None] - pos[None, :]
        mask = (dist >= 0) & (dist < WINDOW) & (pos[None, :] >= 0)
        s = jnp.einsum('bgrqd,bgkd->bgrqk', qc, kw) + shared_bias(dist)
        p = masked_softmax(s, mask)
        o_win = jnp.einsum('bgrqk,bgkd->bgrqd', p.astype(vw.dtype), vw)
        return o_cmp, o_slc, o_win

    starts = jnp.arange(0, S, Q_BLOCK, dtype=jnp.int32)
    outs = lax.map(block_fn, starts)
    o = jnp.stack([ob.transpose(1, 0, 4, 2, 3, 5).reshape(B, S, N_HEADS_2, dh) for ob in outs], axis=2)
    g = jax.nn.sigmoid(br_gate.reshape(B, S, 3, N_HEADS_2, 1))
    return (g * o).sum(axis=2).reshape(B, S, NSA_WIDTH)

def rglru_mixer(u, conv_w, conv_b, lru_wa, lru_ba, lru_wx, lru_bx, lru_lambda):
    B, S, W = u.shape
    up = jnp.pad(u, ((0, 0), (CONV_WIDTH_2 - 1, 0), (0, 0)))
    uc = conv_b + sum(up[:, k:k + S] * conv_w[k] for k in range(CONV_WIDTH_2))
    ub = uc.reshape(B, S, LRU_BLOCKS, LRU_BLOCK_DIM)
    r = jax.nn.sigmoid(jnp.einsum('bsnd,nde->bsne', ub, lru_wa).reshape(B, S, W) + lru_ba)
    i = jax.nn.sigmoid(jnp.einsum('bsnd,nde->bsne', ub, lru_wx).reshape(B, S, W) + lru_bx)
    log_a = (-LRU_C * r.astype(jnp.float32)) * jax.nn.softplus(-lru_lambda.astype(jnp.float32))
    a = jnp.exp(log_a)
    b = jnp.sqrt(-jnp.expm1(2.0 * log_a)) * (i * uc).astype(jnp.float32)
    def comb(left, right):
        a1, b1 = left
        a2, b2 = right
        return a1 * a2, a2 * b1 + b2
    _, h = lax.associative_scan(comb, (a, b), axis=1)
    return h.astype(u.dtype)

def second_block(x, norm_gain, w_in, q_norm_gain, k_norm_gain, cmp_pe, cmp_w1, cmp_b1, cmp_w2, rel_bias,
              conv_w, conv_b, lru_wa, lru_ba, lru_wx, lru_bx, lru_lambda, w_proj_a, w_proj_b, w_out):
    B, S, _ = x.shape
    split_idx = np.cumsum(IN_SIZES)[:-1].tolist()
    for _layer in range(DEPTH_2):
        h = rms_norm(x, norm_gain)
        proj = h @ w_in
        q, kv_all, g_nsa, br_gate, u_lru, g_lru, merge_g = jnp.split(proj, split_idx, axis=-1)
        kv_all = kv_all.reshape(B, S, 6, N_KV_GROUPS, HEAD_DIM)
        y_a = nsa_mixer(q, kv_all[:, :, 0], kv_all[:, :, 1], kv_all[:, :, 2], kv_all[:, :, 3],
                        kv_all[:, :, 4], kv_all[:, :, 5], br_gate, q_norm_gain, k_norm_gain,
                        cmp_pe, cmp_w1, cmp_b1, cmp_w2, rel_bias)
        y_a = (y_a * jax.nn.silu(g_nsa)) @ w_proj_a
        y_b = rglru_mixer(u_lru, conv_w, conv_b, lru_wa, lru_ba, lru_wx, lru_bx, lru_lambda)
        y_b = (y_b * jax.nn.silu(g_lru)) @ w_proj_b
        gate_a, gate_b = jnp.split(merge_g, N_BRANCHES, axis=-1)
        m = jax.nn.sigmoid(gate_a) * y_a + jax.nn.sigmoid(gate_b) * y_b
        x = x + m @ w_out
    return x


def setup_inputs(seed=0):
    out = dict(first_inputs(seed))
    for name, value in second_inputs(seed + 1).items():
        if name != "x":
            out[name + "_2"] = value
    return out


def reference(
    x, norm_mix, w_in, rw_mu, rw_w0, rw_w2, rw_a0, rw_a2, rw_g2, rw_k_k, rw_k_a, rw_r_k,
    rw_ln_w, rw_ln_b, sb_q_norm, sb_k_norm, ret_gn, conv_dw, conv_b, conv_ln_w, conv_ln_b,
    w_gate, w_branch, w_out, norm_ffn, ffn_w1, ffn_w3, ffn_w2, router, moe_w1, moe_w3, moe_w2,
    norm_gain_2, w_in_2, q_norm_gain_2, k_norm_gain_2, cmp_pe_2, cmp_w1_2, cmp_b1_2, cmp_w2_2,
    rel_bias_2, conv_w_2, conv_b_2, lru_wa_2, lru_ba_2, lru_wx_2, lru_bx_2, lru_lambda_2,
    w_proj_a_2, w_proj_b_2, w_out_2,
):
    x = first_block(
        x, norm_mix, w_in, rw_mu, rw_w0, rw_w2, rw_a0, rw_a2, rw_g2, rw_k_k, rw_k_a, rw_r_k,
        rw_ln_w, rw_ln_b, sb_q_norm, sb_k_norm, ret_gn, conv_dw, conv_b, conv_ln_w, conv_ln_b,
        w_gate, w_branch, w_out, norm_ffn, ffn_w1, ffn_w3, ffn_w2, router, moe_w1, moe_w3,
        moe_w2,
    )
    return second_block(
        x, norm_gain_2, w_in_2, q_norm_gain_2, k_norm_gain_2, cmp_pe_2, cmp_w1_2, cmp_b1_2,
        cmp_w2_2, rel_bias_2, conv_w_2, conv_b_2, lru_wa_2, lru_ba_2, lru_wx_2, lru_bx_2,
        lru_lambda_2, w_proj_a_2, w_proj_b_2, w_out_2,
    )


_drawn_inputs = setup_inputs


def setup_inputs(seed=0):
    import zlib

    import numpy as np

    out = dict(_drawn_inputs(seed))
    spreads = {}
    factors = {'rw_w2': 3.013,
     'rw_k_k': 15.136,
     'rw_ln_b': 8.0,
     'sb_q_norm': 3.072,
     'sb_k_norm': 2.737,
     'conv_b': 7.087,
     'conv_ln_b': 8.0,
     'q_norm_gain_2': 8.0,
     'k_norm_gain_2': 8.0,
     'cmp_b1_2': 8.0,
     'lru_ba_2': 64.0,
     'lru_bx_2': 45.236,
     'rel_bias_2': 5.845}
    for name, (base, spread) in spreads.items():
        noise = np.random.default_rng([zlib.crc32(name.encode()), seed]).standard_normal(out[name].shape)
        drawn = base * np.exp(spread * noise) if base else spread * noise
        out[name] = __import__('jax').numpy.asarray(drawn.astype(out[name].dtype))
    for name, factor in factors.items():
        out[name] = (out[name] * factor).astype(out[name].dtype)
    return out
```

```python
import concourse.bass as bass
import numpy as np
from concourse import mybir

F32 = mybir.dt.float32
U32 = mybir.dt.uint32
BF16 = mybir.dt.bfloat16
ALU = mybir.AluOpType
ACT = mybir.ActivationFunctionType
AX = mybir.AxisListType

P = 128
T = 256
TT2 = T // P
D = 1024
KD = D // P
LAYERS = 2
RING = 11
HD = 64
CH = 32
NCH = T // CH
RW_SCALE = 0.606531
NORM_EPS = 1e-6
RW_LN_EPS = 64e-5
GN_EPS = 1e-5
CONV_LN_EPS = 1e-5
TAPS = 31
PAD = TAPS - 1
FF_TILES = 11
MIX_BLOCKS = 77
EXP_BLOCKS = 3 * FF_TILES
SEC_BLOCKS = 66
MIX_ROUNDS = MIX_BLOCKS // RING
EXP_ROUNDS = EXP_BLOCKS // RING
SEC_ROUNDS = SEC_BLOCKS // RING
DENSE_PARTS = 2
EXPERTS = 8
LAYER0_ROUNDS = MIX_ROUNDS + DENSE_PARTS * EXP_ROUNDS
SEC_FIRST_ROUND = 2 * MIX_ROUNDS + (DENSE_PARTS + EXPERTS) * EXP_ROUNDS
NEG = -1e30
BUCKETS = 32
HEADS2 = 8
NC = T // 16 - 1
VEC = 2 * T - 1

PCOL = {}
_at = 0
for _name, _n in [("norm_mix", 8), ("norm_ffn", 8), ("mu", 8), ("w0", 2), ("a0", 2), ("k_k", 2), ("k_a", 2),
                  ("r_k", 2), ("rw_ln_w", 2), ("rw_ln_b", 2), ("sb_q", 1), ("sb_k", 1), ("ret_gn", 2),
                  ("dw", 2 * TAPS), ("conv_b", 2), ("conv_ln_w", 2), ("conv_ln_b", 2), ("is_moe", 1),
                  ("is_dense", 1), ("pad", 1), ("lora", 512), ("router", 64)]:
    PCOL[_name] = (_at, _at + _n)
    _at += _n
PN = _at

QCOL = {}
_at = 0
for _name, _n in [("gain", 8), ("q_gain", 1), ("k_gain", 3), ("b1", 4), ("pe", 32), ("w2", 256), ("conv_w", 16),
                  ("conv_b", 4), ("ba", 4), ("bx", 4), ("lambda", 4), ("wa", 512), ("wx", 512), ("br", 192), ("rel", 8),
                  ("onehot", 2 * VEC), ("cmp_ok", 32)]:
    QCOL[_name] = (_at, _at + _n)
    _at += _n
QN = _at

CCOL = {}
_at = 0
for _name, _n in [("ident", 128), ("flip", 128), ("ones", 128), ("headones", 128), ("swap", 128), ("cos", 256), ("sin", 256),
                  ("decay", 1024), ("strictT", 128), ("negmask", 128), ("negtri", 128), ("negones", 128),
                  ("grams", 512), ("negstrict", 128), ("resets", 256), ("eps", 8), ("iota8", 8)]:
    CCOL[_name] = (_at, _at + _n)
    _at += _n
CN = _at
EPS_COL = {"norm": 0, "sbq": 1, "rwln": 2, "gn": 3, "one": 4}


def constants():
    c = np.zeros((P, CN), np.float32)

    def put(name, a):
        s, e = CCOL[name]
        c[:a.shape[0], s:e] = a.reshape(a.shape[0], e - s)

    i = np.arange(P)
    put("ident", np.eye(P, dtype=np.float32))
    put("flip", np.eye(P, dtype=np.float32)[::-1])
    put("ones", np.ones((P, P), np.float32))
    put("headones", (i[:, None] // HD == i[None, :] // HD).astype(np.float32))
    swap = np.zeros((P, P), np.float32)
    for m in range(P):
        if m % HD < HD // 2:
            swap[m + HD // 2, m] = -1.0
        else:
            swap[m - HD // 2, m] = 1.0
    put("swap", swap)
    inv = np.float32(10000.0) ** (-np.arange(0, HD, 2, dtype=np.float32) / np.float32(HD))
    ang = (np.arange(T, dtype=np.float32)[None, :] * inv.astype(np.float32)[:, None]).astype(np.float32)
    put("cos", np.tile(np.cos(ang.astype(np.float64)), (4, 1)).astype(np.float32))
    put("sin", np.tile(np.sin(ang.astype(np.float64)), (4, 1)).astype(np.float32))
    rel = np.arange(T)[None, :] - i[:, None]
    dec = [np.where(rel >= 0, (1.0 - 2.0 ** (-5.0 - h)) ** np.maximum(rel, 0) * HD ** -0.5, 0.0) for h in range(4)]
    put("decay", np.stack(dec, 1).astype(np.float32))
    put("strictT", (i[:, None] < i[None, :]).astype(np.float32))
    put("negmask", np.where(i[:, None] < i[None, :], 0.0, NEG).astype(np.float32))
    put("negtri", -(i[:, None] >= i[None, :]).astype(np.float32))
    put("negones", -np.ones((P, P), np.float32))
    same = i[:, None] // CH == i[None, :] // CH
    before = (same & (i[:, None] < i[None, :])).astype(np.float32)
    upto = (same & (i[:, None] <= i[None, :])).astype(np.float32)
    put("grams", np.stack([-before, upto, before, upto], 1))
    put("negstrict", -before.T)
    put("resets", np.tile((np.arange(T) % CH != 0).astype(np.float32), (P, 1)))
    put("eps", np.tile(np.array([NORM_EPS, NORM_EPS * HD, RW_LN_EPS, GN_EPS, 1.0, 0, 0, 0], np.float32), (P, 1)))
    put("iota8", np.tile(np.arange(8, dtype=np.float32), (P, 1)))
    return c


class Plan:

    def __init__(self, nc, known):
        self.sem = {e: nc.alloc_semaphore(f"{e}_steps") for e in ("pe", "act", "dve", "pool", "par")}
        self.count = dict.fromkeys(self.sem, 0)
        self.known = known
        self.steps = {}
        self.phase = 0

    def done(self, engine, name=None, by=1):
        self.count[engine] += by
        if name:
            assert (self.phase, name) not in self.steps, name
            self.steps[self.phase, name] = (engine, self.count[engine])
        return self.sem[engine], by

    def after(self, name):
        engine, n = self.known[self.phase, name] if self.known is not None else ("pe", 1)
        return self.sem[engine], n

    def restart(self):
        self.count = dict.fromkeys(self.count, 0)
        self.phase += 1


def program(nc, dram, known):
    plan = Plan(nc, known)
    after, done = plan.after, plan.done
    blk_in = [nc.alloc_semaphore(f"block_in_slot{s}") for s in range(RING)]
    blk_used = nc.alloc_semaphore("blocks_used")
    sb = lambda name, *dims: nc.alloc_sbuf_tensor(name, [P, int(np.prod(dims))], F32)[:, :]

    ring = sb("ring", RING, D).rearrange("p (s n) -> p s n", s=RING)
    cst = sb("cst", CN)
    x = sb("x_chan", KD, T).rearrange("p (k t) -> p k t", k=KD)
    h = sb("h_chan", KD, T).rearrange("p (k t) -> p k t", k=KD)
    arena = sb("arena", 53100 - RING * D - CN - 2 * KD * T)
    banks = {n: nc.alloc_psum_tensor(f"bank_{n}", [P, 512], F32)[:, :] for n in ("P0", "P1", "Z0", "Z1", "O", "C", "Y", "X")}

    def col(src, table, name, i=0, n=None):
        s, e = table[name]
        return src[:, s + i:(s + i + n) if n else e]

    C = lambda name, i=0, n=None: col(cst, CCOL, name, i, n)
    eps = lambda name: C("eps", EPS_COL[name], 1)
    ident = C("ident")

    env = dict(nc=nc, plan=plan, after=after, done=done, blk_in=blk_in, blk_used=blk_used, ring=ring, cst=cst, x=x,
               h=h, arena=arena, banks=banks, C=C, eps=eps, ident=ident, dram=dram, col=col)

    loop_sems = {}

    def sem(name):
        if name not in loop_sems:
            loop_sems[name] = nc.alloc_semaphore(name)
        return loop_sems[name]

    env.update(sem=sem, loop_sems=loop_sems)
    load_phase(env)
    with nc.Fori(0, LAYERS) as layer:
        mix_phase(env, layer)
        ffn_phase(env, layer)
    second_phase(env)
    return plan.steps


def phase_end(env):
    nc, plan = env["nc"], env["plan"]
    nc.all_engine_barrier()
    for s in [*plan.sem.values(), *env["loop_sems"].values()]:
        nc.sync.sem_clear(s)
    nc.all_engine_barrier()
    plan.restart()


def carver(env):
    at = [0]

    def cut(*dims):
        n = int(np.prod(dims))
        a = env["arena"][:, at[0]:at[0] + n]
        at[0] += n
        assert at[0] <= env["arena"].shape[1], at[0]
        if len(dims) == 2:
            a = a.rearrange("p (a b) -> p a b", a=dims[0])
        elif len(dims) == 3:
            a = a.rearrange("p (a b c) -> p a b c", a=dims[0], b=dims[1])
        elif len(dims) == 4:
            a = a.rearrange("p (a b c d) -> p a b c d", a=dims[0], b=dims[1], c=dims[2])
        elif len(dims) == 5:
            a = a.rearrange("p (a b c d e) -> p a b c d e", a=dims[0], b=dims[1], c=dims[2], d=dims[3])
        return a

    cut.at = at
    return cut


def load_rounds(env, sp, first, count):
    with sp.Fori(0, count) as i:
        for s in range(RING):
            block = sp.snap((first + i) * RING + s)
            need = sp.snap((first + i - 1) * RING + s + 1)
            sp.wait_ge(env["blk_used"], need)
            sp.wait_ge(env["blk_used"], 1)
            sp.dma_start(env["ring"][:, s, :], env["dram"]["stream"][block]).then_inc(env["blk_in"][s], 16)


class Blocks:

    def __init__(self, env, pe, first):
        self.env, self.pe, self.first, self.n, self.unreleased = env, pe, first, 0, 0

    def next(self):
        slot, r = self.n % RING, self.n // RING
        self.pe.wait_ge(self.env["blk_in"][slot], self.pe.snap((self.first + (r + 1)) * 16))
        self.n += 1
        return self.env["ring"][:, slot, :]

    def col(self):
        return self.next().rearrange("p (k n) -> p k n", k=KD)

    def release(self, mm):
        if self.unreleased:
            mm.then_inc(self.env["blk_used"], self.unreleased)
            self.unreleased = 0

    def flush(self, padding=0):
        for _ in range(padding):
            self.next()
        self.unreleased += padding
        self.release(self.pe.matmul(self.env["banks"]["X"][0:1, 0:1], self.env["ident"][0:1, 0:1],
                                    self.env["ident"][0:1, 0:1], start=True, stop=True))


def load_phase(env):
    nc, dram, x, ring, banks = env["nc"], env["dram"], env["x"], env["ring"], env["banks"]
    after, done, ident = env["after"], env["done"], env["ident"]
    cut = carver(env)
    xin = cut(TT2, D)
    with nc.Block() as block:
        @block.sync
        def _(sp):
            sp.dma_start(xin, dram["x"].rearrange("o (a p) d -> p (o a) d", p=P)).then_inc(*done("par", by=16))
            sp.dma_start(env["cst"], dram["consts"]).then_inc(*done("par", "loaded", by=16))
            for s in range(RING):
                sp.dma_start(ring[:, s, :], dram["stream"][s]).then_inc(env["blk_in"][s], 16)

        @block.tensor
        def _(pe):
            pe.wait_ge(*after("loaded"))
            for k in range(KD):
                if k >= 2:
                    pe.wait_ge(*after(f"x_{k - 2}"))
                for a in range(TT2):
                    mm = pe.transpose(banks[f"P{k % 2}"][:, a * P:(a + 1) * P], xin[:, a, k * P:(k + 1) * P], ident)
                mm.then_inc(*done("pe", f"xT_{k}"))

        @block.vector
        def _(v):
            for k in range(KD):
                v.wait_ge(*after(f"xT_{k}"))
                v.tensor_copy(x[:, k, :], banks[f"P{k % 2}"][:, 0:T]).then_inc(*done("dve", f"x_{k}"))
    phase_end(env)


def mix_phase(env, layer):
    nc, dram, x, h, banks = env["nc"], env["dram"], env["x"], env["h"], env["banks"]
    after, done, C, eps, ident, col, plan = (env[n] for n in ("after", "done", "C", "eps", "ident", "col", "plan"))
    first_round = nc.snap(layer * LAYER0_ROUNDS)
    P0, P1, Z0, Z1, BO, BC, BY, BX = (banks[n] for n in ("P0", "P1", "Z0", "Z1", "O", "C", "Y", "X"))
    pair = lambda b: b.rearrange("p (j t) -> p j t", j=2)
    quad = lambda b: b.rearrange("p (j t) -> p j t", j=4)

    cut = carver(env)
    prm = cut(PN)
    R = lambda name, i=0, n=1: col(prm, PCOL, name, i, n)
    merged = cut(KD, T)
    gates = cut(2, KD, T)
    KR = cut(2, NCH, 2, P)
    BK = cut(2, 2, NCH, P)
    Vst = cut(NCH, HD)
    region_at = cut.at[0]
    G = cut(NCH, 4, P)
    M = cut(2, 4, P)
    MT = cut(2, 4, P)
    TI = cut(NCH, P)
    region_end = cut.at[0]
    yst, ysq = (M[:, i].rearrange("p a n -> p (a n)").rearrange("p (c v) -> p c v", c=NCH) for i in range(2))
    yT = MT[:, 0].rearrange("p a n -> p (a n)").rearrange("p (j t) -> p j t", j=2)
    cut.at[0] = region_at
    praw = cut(8, T + 1)
    pm = cut(6, T)
    sig, av, cumL, eP, eN, eM, kk = (cut(2, T) for _ in range(7))
    assert cut.at[0] <= region_end + 512, (cut.at[0], region_end)
    cut.at[0] = max(cut.at[0], region_end)
    pv = praw.rearrange("p a b -> p (a b)")
    kp, kn, prev, sbn = (pv[:, i * 512:(i + 1) * 512].rearrange("p (j t) -> p j t", j=2) for i in range(4))
    A1 = cut(4, P)
    vv, gg, bonus, sbq, sbk, sbo, sbv, rv, rg, acc, scr = (cut(2, T) for _ in range(11))
    u = cut(2, PAD + T)
    az, at_, exz = cut(384), cut(384), cut(384)
    S = cut(2, 2, HD)
    Se = cut(2, HD)
    dec = cut(2, NCH)
    rhsn, sa, w0h, small = cut(HD), cut(HD), cut(4), cut(64)
    mview = merged.rearrange("p k t -> p (k t)")
    rq, rkk, rqr, rkr = (mview[:, i * 512:(i + 1) * 512].rearrange("p (j t) -> p j t", j=2) for i in range(4))
    sqx = merged
    flat = lambda a: a.rearrange("p j t -> p (j t)")

    with nc.Block() as block:
        @block.sync
        def _(sp):
            sp.dma_start(prm, dram["params"][layer]).then_inc(*done("par", "params", by=16))
            load_rounds(env, sp, sp.snap(first_round + 1), MIX_ROUNDS)

        @block.gpsimd
        def _(g):
            g.memset(praw[:, :, 0:1], 0.0).then_inc(*done("pool", "praw_zeroed"))
            g.memset(KR, 0.0).then_inc(*done("pool"))
            g.memset(BK, 0.0).then_inc(*done("pool"))
            g.memset(u[:, :, 0:PAD], 0.0).then_inc(*done("pool", "zeroed"))

        @block.tensor
        def _(pe):
            blocks = Blocks(env, pe, first_round)

            def project(bank, j, name=None):
                w = blocks.col()
                for k in range(KD):
                    mm = pe.matmul(bank[:, j * T:(j + 1) * T], w[:, k, :], h[:, k, :], start=(k == 0), stop=(k == KD - 1))
                    if k == 0:
                        blocks.release(mm)
                blocks.unreleased += 1
                return mm

            def project_tm(bank, j):
                w = blocks.col()
                b = pair(bank)
                for a in range(TT2):
                    for k in range(KD):
                        mm = pe.matmul(b[:, a, j * P:(j + 1) * P], h[:, k, a * P:(a + 1) * P], w[:, k, :],
                                       start=(k == 0), stop=(k == KD - 1))
                        if k == 0 and a == 0:
                            blocks.release(mm)
                blocks.unreleased += 1
                return mm

            pe.wait_ge(*after("sqx"))
            for k in range(KD):
                mm = pe.matmul(BX[:, 0:T], C("ones"), sqx[:, k, :], start=(k == 0), stop=(k == KD - 1))
            mm.then_inc(*done("pe", "ssx"))

            bank_of = [P0, P1]
            readers = {}

            def take(bank, reader):
                if bank.tensor.name in readers:
                    pe.wait_ge(*after(readers[bank.tensor.name]))
                readers[bank.tensor.name] = reader

            names = ["rw_raw0", "rw_raw1", "rw_raw2", "rw_raw3", "sbq_raw", "sbk_raw", "sbv", "rq_raw", "rk_raw", "rv", "rg",
                     "conv_a", "conv_b"]
            turn = [0]

            def in_proj(name):
                bank = bank_of[turn[0] % 2]
                turn[0] += 1
                take(bank, name)
                for j in range(2):
                    if turn[0] == 1 and j == 0:
                        pe.wait_ge(*after("h"))
                    mm = (project_tm if name in ("sbv", "rv") else project)(bank, j)
                mm.then_inc(*done("pe", "p_" + name))

            for name in names[:4]:
                in_proj(name)
            in_proj("sbq_raw")
            take(Z0, "thw")
            pe.wait_ge(*after("lora_w_in"))
            for j in range(2):
                mm = pe.matmul(Z0[:, j * T:(j + 1) * T], R("lora", j * P, P)[0:64, :], pm[0:64, 4, :], start=True, stop=True)
            mm.then_inc(*done("pe", "lora_w"))
            take(Z1, "tha")
            for j in range(2):
                mm = pe.matmul(Z1[:, j * T:(j + 1) * T], R("lora", j * P, P)[64:128, :], pm[64:128, 4, :], start=True,
                               stop=True)
            mm.then_inc(*done("pe", "lora_a"))
            take(BX, "kk_norm")
            pe.wait_ge(*after("kk_sq"))
            pe.matmul(BX, C("headones"), flat(scr), start=True, stop=True).then_inc(*done("pe", "kk_ss"))
            in_proj("sbk_raw")
            take(BO, "g")
            pe.wait_ge(*after("lora_g_in"))
            for j in range(2):
                mm = pe.matmul(BO[:, j * T:(j + 1) * T], R("lora", 256 + j * P, P), pm[:, 5, :], start=True, stop=True)
            mm.then_inc(*done("pe", "lora_g"))
            in_proj("sbv")
            in_proj("rq_raw")
            in_proj("rk_raw")
            take(BC, "bonus")
            pe.wait_ge(*after("rkr"))
            pe.matmul(BC, C("headones"), flat(scr), start=True, stop=True).then_inc(*done("pe", "rkr_sum"))
            in_proj("rv")
            take(BY, "Vst")
            for a in range(TT2):
                for j in range(2):
                    mm = pe.transpose(BY[:, (2 * a + j) * P:(2 * a + j + 1) * P], vv[:, j, a * P:(a + 1) * P], ident)
            mm.then_inc(*done("pe", "vT"))
            in_proj("rg")
            take(BX, "sbq_rms")
            pe.wait_ge(*after("sbq_sq"))
            pe.matmul(BX, C("headones"), flat(sbo), start=True, stop=True).then_inc(*done("pe", "sbq_ss"))
            in_proj("conv_a")
            take(BX, "sbk_rms")
            pe.wait_ge(*after("sbk_sq"))
            pe.matmul(BX, C("headones"), flat(sbo), start=True, stop=True).then_inc(*done("pe", "sbk_ss"))
            in_proj("conv_b")
            take(BO, "rot_q")
            pe.wait_ge(*after("rq_raw"))
            pe.matmul(BO, C("swap"), flat(rq), start=True, stop=True).then_inc(*done("pe", "swap_q"))
            take(BC, "rot_k")
            pe.wait_ge(*after("rk_raw"))
            pe.matmul(BC, C("swap"), flat(rkk), start=True, stop=True).then_inc(*done("pe", "swap_k"))

            def gate(n):
                if n % 2 == 0:
                    bank = bank_of[turn[0] % 2]
                    take(bank, f"gate_{n // 2}")
                bank = bank_of[turn[0] % 2]
                mm = project(bank, n % 2)
                if n % 2:
                    turn[0] += 1
                    mm.then_inc(*done("pe", f"p_gate_{n // 2}"))

            def apply(branch, y, ready):
                pe.wait_ge(*after(ready))
                w = [blocks.next(), blocks.next()]
                for q in range(4):
                    bank = bank_of[turn[0] % 2]
                    turn[0] += 1
                    take(bank, f"applied_{branch}_{q}")
                    for j in range(2):
                        d = 2 * q + j
                        for c in range(2):
                            mm = pe.matmul(bank[:, j * T:(j + 1) * T], w[c][:, d * P:(d + 1) * P], y[:, c, :],
                                           start=(c == 0), stop=(c == 1))
                            if c == 0:
                                blocks.release(mm)
                    mm.then_inc(*done("pe", f"p_{branch}_{q}"))
                blocks.unreleased += 2

            def gram(c):
                z = Z0 if c % 2 == 0 else Z1
                take(z, f"gram_{c}")
                for w in range(2):
                    for j in range(2):
                        mm = pe.matmul(z[:, w * T:(w + 1) * T], BK[:, w, j, c, :],
                                       KR[:, j, c].rearrange("p w n -> p (w n)"), start=(j == 0), stop=(j == 1))
                mm.then_inc(*done("pe", f"p_gram_{c}"))
                if c % 4 == 0:
                    take(BX, f"A_{c // 4}")
                for j in range(2):
                    mm = pe.matmul(quad(BX)[:, c % 4, :], KR[:, j, c, 0, :], BK[:, 0, j, c, :], start=(j == 0), stop=(j == 1))
                if c % 4 == 3:
                    mm.then_inc(*done("pe", f"p_A_{c // 4}"))
                o = BO if c % 2 == 0 else BC
                take(o, f"BK_{c}")
                for w in range(2):
                    for j in range(2):
                        mm = pe.transpose(quad(o)[:, 2 * w + j, :], BK[:, w, j, c, :], ident)
                mm.then_inc(*done("pe", f"p_BK_{c}"))

            pe.wait_ge(*after("expanded"))
            for c in range(NCH):
                gram(c)
                gate(c)

            def mt_of(g, k):
                return [G[:, 4 * g + i, 0, :] for i in range(4)] if k == 0 else [MT[:, k % 2, i, :] for i in range(4)]

            def squares(g, k):
                pe.wait_ge(*after(f"M_{g}_{k - 1}" if k > 1 else f"A_{g}"))
                if k > 1:
                    pe.wait_ge(*after(f"MT_{g}_{k - 1}"))
                mt = mt_of(g, k - 1)
                m = [(A1 if g and k == 1 else M[:, (k - 1) % 2])[:, i, :] for i in range(4)]
                take(BC, f"M_{g}_{k}")
                for i in range(4):
                    mm = pe.matmul(quad(BC)[:, i, :], mt[i], m[i], start=True, stop=True)
                mm.then_inc(*done("pe", f"p_M_{g}_{k}"))
                if k < 4:
                    take(BX, f"MT_{g}_{k}")
                    for i in range(4):
                        mm = pe.matmul(quad(BX)[:, i, :], m[i], mt[i], start=True, stop=True)
                    mm.then_inc(*done("pe", f"p_MT_{g}_{k}"))

            def inverse(g, k):
                pe.wait_ge(*after(f"M_{g}_{k}"))
                pe.wait_ge(*after(f"TI_{g}_{k - 1}"))
                take(BY, f"TI_{g}_{k}")
                for i in range(4):
                    mm = pe.matmul(quad(BY)[:, i, :], M[:, k % 2, i, :], TI[:, 4 * g + i, :], start=True, stop=True)
                mm.then_inc(*done("pe", f"p_TI_{g}_{k}"))

            def ret_scores(hh):
                z = Z0 if hh % 2 == 0 else Z1
                b, j = (hh % 2) * HD, hh // 2
                take(z, f"ret_s_{hh}")
                pe.matmul(z[:, 0:T], rkr[b:b + HD, j, 0:P], rqr[b:b + HD, j, :], start=True, stop=True)
                pe.matmul(z[:, T:T + P], rkr[b:b + HD, j, P:T], rqr[b:b + HD, j, P:T], start=True, stop=True)\
                  .then_inc(*done("pe", f"p_ret_s_{hh}"))

            def attend(hh, values, weights, ready, out_name):
                b, j = (hh % 2) * HD, hh // 2
                pe.wait_ge(*after(ready))
                pe.matmul(BO[b:b + HD, j * T:(j + 1) * T], values[:, 0, hh * HD:(hh + 1) * HD], weights[:, 0:T],
                          start=True, stop=False, skip_group_check=True)
                pe.matmul(BO[b:b + HD, j * T + P:(j + 1) * T], values[:, 1, hh * HD:(hh + 1) * HD], weights[:, T:T + P],
                          start=False, stop=True, skip_group_check=True).then_inc(*done("pe", out_name))

            pe.wait_ge(*after("rot_k"))
            pe.wait_ge(*after("rv"))
            ret_scores(0)
            squares(0, 1)
            gate(8)
            take(BO, "ret_o")
            for k in range(1, 5):
                inverse(0, k)
                if k < 4:
                    squares(0, k + 1)
                attend(k - 1, rv, az if k % 2 else at_, f"ret_s_{k - 1}", f"p_ret_o_{k - 1}")
                if k < 4:
                    ret_scores(k)
                gate(8 + k)
            squares(1, 1)
            gate(13)
            take(Z0, "ret_xc")
            pe.wait_ge(*after("ret_o"))
            pe.matmul(Z0, C("headones"), flat(rq), start=True, stop=True).then_inc(*done("pe", "ret_sum"))
            inverse(1, 1)
            squares(1, 2)
            gate(14)
            take(Z1, "ret_std")
            pe.wait_ge(*after("ret_sq"))
            pe.matmul(Z1, C("headones"), flat(scr), start=True, stop=True).then_inc(*done("pe", "ret_ss"))
            inverse(1, 2)
            squares(1, 3)
            gate(15)
            take(Z0, "conv_xc")
            pe.wait_ge(*after("conv_y"))
            for j in range(2):
                mm = pe.matmul(Z0[:, 0:T], C("ones"), acc[:, j, :], start=(j == 0), stop=(j == 1))
            mm.then_inc(*done("pe", "conv_sum"))
            inverse(1, 3)
            squares(1, 4)
            take(Z1, "conv_std")
            pe.wait_ge(*after("conv_sq"))
            for j in range(2):
                mm = pe.matmul(Z1[:, 0:T], C("ones"), scr[:, j, :], start=(j == 0), stop=(j == 1))
            mm.then_inc(*done("pe", "conv_ss"))
            inverse(1, 4)
            apply("conv", acc, "conv_out")
            apply("ret", rg, "ret_out")

            def sb_z(hh):
                z = Z0 if hh % 2 == 0 else Z1
                b, j = (hh % 2) * HD, hh // 2
                take(z, f"sb_sp_{hh}")
                pe.matmul(z[:, 0:T], sbk[b:b + HD, j, 0:P], sbq[b:b + HD, j, :], start=True, stop=False,
                          skip_group_check=True)
                pe.matmul(z[:, T:T + P], sbk[b:b + HD, j, P:T], sbq[b:b + HD, j, P:T], start=False, stop=True,
                          skip_group_check=True).then_inc(*done("pe", f"sb_z_{hh}"))

            def sb_cum(hh):
                z = Z0 if hh % 2 == 0 else Z1
                take(z, f"sb_a_{hh}")
                pe.matmul(z[:, 0:T], C("negtri"), az[:, 0:T], start=False, stop=False, skip_group_check=True)
                pe.matmul(z[:, T:T + P], C("negtri"), az[:, T:T + P], start=False, stop=False, skip_group_check=True)
                pe.matmul(z[:, P:T], C("negones"), az[:, T:T + P], start=False, stop=False, skip_group_check=True)
                pe.matmul(z[:, 0:P], ident, C("negmask"), start=False, stop=False, skip_group_check=True)
                pe.matmul(z[:, T:T + P], ident, C("negmask"), start=False, stop=True, skip_group_check=True)\
                  .then_inc(*done("pe", f"sb_cum_{hh}"))

            def scan_rhs(c):
                take(BC, f"rhs_{c}")
                if c:
                    pe.wait_ge(*after(f"S_{c}"))
                    for j in range(2):
                        pe.matmul(BC[:, 0:HD], KR[:, j, c, 0, :], S[:, c % 2, j, :], start=(j == 0), stop=False)
                pe.matmul(BC[:, 0:HD], G[:, c, 2, :], Vst[:, c, :], start=(c == 0), stop=True)\
                  .then_inc(*done("pe", f"p_rhs_{c}"))

            def scan_sa(c):
                take(BC, f"sa_{c}")
                pe.matmul(BC[:, HD:2 * HD], TI[:, c, :], rhsn, start=True, stop=True).then_inc(*done("pe", f"p_sa_{c}"))

            def scan_state(c):
                pe.wait_ge(*after(f"sa_{c}"))
                if c < NCH - 1:
                    take(BC, f"S_{c + 1}")
                    for j in range(2):
                        o = BC[:, (2 + j) * HD:(3 + j) * HD]
                        pe.matmul(o, BK[:, 0, j, c, :], sa, start=True, stop=False)
                        mm = pe.matmul(o, BK[:, 1, j, c, :], Vst[:, c, :], start=False, stop=True)
                    mm.then_inc(*done("pe", f"p_S_{c + 1}"))
                y = BY[:, c * HD:(c + 1) * HD]
                if c:
                    for j in range(2):
                        pe.matmul(y, KR[:, j, c, 1, :], S[:, c % 2, j, :], start=(j == 0), stop=False)
                pe.matmul(y, G[:, c, 1, :], sa, start=(c == 0), stop=False)
                pe.matmul(y, G[:, c, 3, :], Vst[:, c, :], start=False, stop=True).then_inc(*done("pe", f"p_y_{c}"))

            take(BY, "y")
            pe.wait_ge(*after("TI_1_4"))
            pe.wait_ge(*after("Vst"))
            pe.wait_ge(*after("sbk_n"))
            take(BO, "sb_out")
            for c in range(NCH):
                hh = c // 2
                scan_rhs(c)
                if c % 2 == 0:
                    sb_z(hh)
                gate(16 + 2 * c)
                scan_sa(c)
                if c % 2 == 1:
                    sb_cum(hh)
                gate(17 + 2 * c)
                scan_state(c)
                if c % 2 == 1:
                    attend(hh, sbv, at_, f"sb_a_{hh}", f"sb_o_{hh}")
            apply("sb", sbo, "sb_out")
            for a in range(2):
                bank = (Z0, Z1)[a]
                take(bank, f"yT_{a}")
                pe.wait_ge(*after("yn"))
                for i in range(4):
                    mm = pe.transpose(bank[0:HD, i * P:(i + 1) * P], yst[:, 4 * a + i, :], ident)
                mm.then_inc(*done("pe", f"p_yT_{a}"))
            apply("rw", gg, "rw_out")
            pe.wait_ge(*after("merged"))
            for q in range(4):
                bank = bank_of[turn[0] % 2]
                turn[0] += 1
                take(bank, f"x_{q}")
                for j in range(2):
                    w = blocks.col()
                    for k in range(KD):
                        mm = pe.matmul(bank[:, j * T:(j + 1) * T], w[:, k, :], merged[:, k, :], start=(k == 0),
                                       stop=(k == KD - 1))
                        if k == 0:
                            blocks.release(mm)
                    blocks.unreleased += 1
                mm.then_inc(*done("pe", f"p_x_{q}"))
            pe.wait_ge(*after("all_read"))
            blocks.flush(padding=3)

        @block.scalar
        def _(a):
            def link(ins, name=None):
                ins.then_inc(*done("act", name))
                a.wait_ge(plan.sem["act"], plan.count["act"])

            def act(out, in_, func, name=None, **kw):
                link(a.activation(out, in_, func, **kw), name)

            act(sqx, x, ACT.Square, "sqx")
            a.wait_ge(*after("ssx"))
            act(az[:, 0:T], BX[:, 0:T], ACT.Sqrt, "x_rms", scale=1.0 / D, bias=eps("norm"))
            for q in range(4):
                a.wait_ge(*after(f"p_rw_raw{q}"))
                act(praw[:, 2 * q:2 * q + 2, 1:T + 1], pair((P0, P1)[q % 2]), ACT.Copy, f"rw_raw{q}")
            a.wait_ge(*after("kkr"))
            act(scr, kk, ACT.Square, "kk_sq")
            a.wait_ge(*after("p_sbq_raw"))
            act(sbq, pair(P0), ACT.Copy, "sbq_raw")
            act(sbo, sbq, ACT.Square, "sbq_sq")
            act(pm[0:64, 4, :], pm[0:64, 4, :], ACT.Tanh, "lora_w_in")
            act(pm[:, 5, :], pm[:, 5, :], ACT.Tanh, "lora_g_th", scale=0.5)
            a.wait_ge(*after("w0h"))
            a.wait_ge(*after("lora_w"))
            for j in range(2):
                act(sig[:, j, :], Z0[:, j * T:(j + 1) * T], ACT.Tanh, "thw" if j else None, scale=0.5, bias=w0h[:, j:j + 1])
            a.wait_ge(*after("lora_a"))
            for j in range(2):
                act(av[:, j, :], Z1[:, j * T:(j + 1) * T], ACT.Tanh, "tha" if j else None, scale=0.5,
                    bias=w0h[:, 2 + j:3 + j])
            a.wait_ge(*after("kk_ss"))
            act(kn, pair(BX), ACT.Sqrt, "kk_norm")
            a.wait_ge(*after("p_sbk_raw"))
            act(sbk, pair(P1), ACT.Copy, "sbk_raw")
            a.wait_ge(*after("lora_g"))
            act(gg, pair(BO), ACT.Copy, "g")
            a.wait_ge(*after("cum"))
            act(eP, cumL, ACT.Exp, scale=-RW_SCALE)
            act(eN, cumL, ACT.Exp, scale=RW_SCALE)
            act(eM, prev, ACT.Exp, "decays", scale=-RW_SCALE)
            for name, out, b in (("sbv", sbv, P0), ("rq_raw", rq, P1), ("rk_raw", rkk, P0), ("rv", rv, P1), ("rg", rg, P0)):
                a.wait_ge(*after("p_" + name))
                act(out, pair(b), ACT.Copy, name)
            act(acc, rg, ACT.Tanh, "rg_th", scale=0.5)
            a.wait_ge(*after("sbq_ss"))
            act(sbn, pair(BX), ACT.Sqrt, "sbq_rms", bias=eps("sbq"))
            act(sbo, sbk, ACT.Square, "sbk_sq")
            a.wait_ge(*after("p_conv_a"))
            act(u[:, :, PAD:PAD + T], pair(P1), ACT.Copy, "conv_a")
            a.wait_ge(*after("sbk_ss"))
            a.wait_ge(*after("sbq_n"))
            act(sbn, pair(BX), ACT.Sqrt, "sbk_rms", scale=1.0 / HD, bias=eps("norm"))
            a.wait_ge(*after("p_conv_b"))
            a.wait_ge(*after("rg_silu"))
            act(acc, pair(P0), ACT.Tanh, "conv_b", scale=0.5)

            def gate(q):
                slot, d = (q // 4) % 2, 2 * (q % 4)
                a.wait_ge(*after(f"p_gate_{q}"))
                if q >= 8:
                    a.wait_ge(*after(f"applied_{('conv', 'ret')[slot]}_3"))
                act(gates[:, slot, d:d + 2, :], pair((P1, P0)[gturn(q) % 2]), ACT.Tanh, f"gate_{q}", scale=0.5)

            gturn = lambda q: q if q < 8 else q + 8
            for c in range(NCH):
                a.wait_ge(*after(f"p_BK_{c}"))
                act(BK[:, :, :, c, :], quad((BO, BC)[c % 2]).rearrange("p (w j) n -> p w j n", w=2), ACT.Copy, f"BK_{c}")
                if c % 2:
                    gate(c // 2)

            def m_copy(g, k):
                a.wait_ge(*after(f"p_M_{g}_{k}"))
                act(M[:, k % 2], quad(BC), ACT.Copy, f"M_{g}_{k}")

            m_copy(0, 1)
            for k in range(1, 5):
                if k < 4:
                    m_copy(0, k + 1)
                if k in (1, 3):
                    gate(4 + k // 2)
            a.wait_ge(*after("p_ret_o_3"))
            m_copy(1, 1)
            act(rq, pair(BO), ACT.Copy, "ret_o")
            gate(6)
            a.wait_ge(*after("ret_xc"))
            act(scr, rkk, ACT.Square, "ret_sq")
            m_copy(1, 2)
            a.wait_ge(*after("ret_ss"))
            act(rq, pair(Z1), ACT.Sqrt, "ret_std", scale=1.0 / HD, bias=eps("gn"))
            m_copy(1, 3)
            gate(7)
            a.wait_ge(*after("conv_xc"))
            act(scr, acc, ACT.Square, "conv_sq")
            m_copy(1, 4)
            a.wait_ge(*after("conv_ss"))
            act(at_[:, 0:T], Z1[:, 0:T], ACT.Sqrt, "conv_std", scale=1.0 / T, bias=eps("gn"))
            a.wait_ge(*after("conv_lin"))
            act(scr, acc, ACT.Tanh, "conv_th", scale=0.5)
            for c in range(NCH):
                hh = c // 2
                if c % 2 == 0:
                    a.wait_ge(*after(f"sb_z_{hh}"))
                    act(exz, (Z0, Z1)[hh % 2][:, 0:384], ACT.Abs)
                    act(exz, exz, ACT.Exp, scale=-1.0)
                    act(exz, exz, ACT.Ln, f"sb_ln_{hh}", bias=eps("one"))
                gate(8 + c)
                if c % 2 == 1:
                    a.wait_ge(*after(f"sb_cum_{hh}"))
                    if hh:
                        a.wait_ge(*after(f"sb_o_{hh - 1}"))
                    act(at_, (Z0, Z1)[hh % 2][:, 0:384], ACT.Exp, f"sb_a_{hh}")
            a.wait_ge(*after("sb_o_3"))
            act(sbo, pair(BO), ACT.Copy, "sb_out")
            a.wait_ge(*after("y_var"))
            act(small[:, 8:16], small[:, 0:8], ACT.Sqrt, "y_std", scale=1.0 / HD, bias=eps("rwln"))

        @block.vector
        def _(v):
            def link(ins, name=None):
                ins.then_inc(*done("dve", name))
                v.wait_ge(plan.sem["dve"], plan.count["dve"])

            tt = lambda out, a0, a1, op, name=None: link(v.tensor_tensor(out, a0, a1, op), name)
            ts = lambda out, a0, s1, s2, op0, op1=None, name=None: link(
                v.tensor_scalar(out, a0, s1, s2, op0) if op1 is None else v.tensor_scalar(out, a0, s1, s2, op0, op1), name)
            stt = lambda out, a0, s, a1, op0, op1, name=None: link(
                v.scalar_tensor_tensor(out=out, in0=a0, scalar=s, in1=a1, op0=op0, op1=op1), name)
            MUL, ADD, SUB, MAX = ALU.mult, ALU.add, ALU.subtract, ALU.max

            v.wait_ge(*after("params"))
            v.wait_ge(*after("x_rms"))
            link(v.reciprocal(az[:, 0:T], az[:, 0:T]))
            for k in range(KD):
                stt(h[:, k, :], x[:, k, :], R("norm_mix", k), az[:, 0:T], MUL, MUL, "h" if k == KD - 1 else None)
            ts(w0h, R("w0", 0, 4), 0.5, None, MUL, name="w0h")
            v.wait_ge(*after("praw_zeroed"))
            for q in range(4):
                v.wait_ge(*after(f"rw_raw{q}"))
                tt(scr, praw[:, 2 * q:2 * q + 2, 0:T], praw[:, 2 * q:2 * q + 2, 1:T + 1], SUB)
                for j in range(2):
                    out = vv[:, j, :] if q == 2 else pm[:, 2 * q + j - (2 if q == 3 else 0), :]
                    stt(out, scr[:, j, :], R("mu", 2 * q + j), praw[:, 2 * q + j, 1:T + 1], MUL, ADD,
                        "v" if q == 2 and j else None)
            for j in range(2):
                ts(kk[:, j, :], pm[:, 2 + j, :], R("k_k", j), None, MUL, name="kkr" if j else None)
            v.wait_ge(*after("lora_g_th"))
            ts(pm[:, 5, :], pm[:, 5, :], 0.5, 0.5, MUL, ADD, name="lora_g_in")
            v.wait_ge(*after("thw"))
            ts(sig, sig, 0.5, 0.5, MUL, ADD)
            for j in range(2):
                link(v.tensor_tensor_scan(cumL[:, j, :], C("resets"), sig[:, j, :], 0.0, MUL, ADD))
            tt(prev, cumL, sig, SUB, "cum")
            v.wait_ge(*after("tha"))
            ts(av, av, 0.5, 0.5, MUL, ADD)
            for j in range(2):
                ts(kp[:, j, :], av[:, j, :], 1.0, R("k_a", j), SUB, MUL)
            stt(kp, kp, 1.0, pm[:, 2:4, :], ADD, MUL)
            v.wait_ge(*after("kk_norm"))
            for j in range(2):
                stt(scr[:, j, :], pm[:, j, :], R("r_k", j), kp[:, j, :], MUL, MUL, "rkr" if j else None)
            ts(kn, kn, 1e-12, None, MAX)
            link(v.reciprocal(kn, kn))
            tt(kk, kk, kn, MUL)
            v.wait_ge(*after("decays"))
            link(v.tensor_copy(dec, eP.rearrange("p j (c t) -> p j c t", c=NCH)[:, :, :, CH - 1]))
            tt(av, av, eN, MUL)
            v.wait_ge(*after("zeroed"))
            chunks = lambda a, j, b: a[b:b + HD, j, :].rearrange("p (c t) -> p c t", c=NCH)
            for hh in range(4):
                j, b, c0 = hh // 2, (hh % 2) * HD, hh * CH
                tt(KR[b:b + HD, j, :, 0, c0:c0 + CH], chunks(kk, j, b), chunks(eM, j, b), MUL)
                tt(KR[b:b + HD, j, :, 1, c0:c0 + CH], chunks(pm, j, b), chunks(eP, j, b), MUL)
                tt(BK[b:b + HD, 0, j, :, c0:c0 + CH], chunks(kk, j, b), chunks(av, j, b), MUL)
                tt(BK[b:b + HD, 1, j, :, c0:c0 + CH], chunks(kp, j, b), chunks(eN, j, b), MUL,
                   "expanded" if hh == 3 else None)
            v.wait_ge(*after("rkr_sum"))
            tt(bonus, pair(BC), vv, MUL, "bonus")
            v.wait_ge(*after("vT"))
            for c4 in range(4):
                for hh in range(4):
                    src = BY[c4 * CH:(c4 + 1) * CH, :].rearrange("p (a n) -> p a n", a=2)[:, :, hh * HD:(hh + 1) * HD]
                    dst = Vst[hh * CH:(hh + 1) * CH].rearrange("p (a c) n -> p a c n", a=2)[:, :, c4, :]
                    link(v.tensor_copy(dst, src), "Vst" if (c4, hh) == (3, 3) else None)
            v.wait_ge(*after("rg_th"))
            ts(acc, acc, 0.5, 0.5, MUL, ADD)
            tt(rg, rg, acc, MUL, "rg_silu")
            v.wait_ge(*after("sbq_rms"))
            link(v.reciprocal(sbn, sbn))
            stt(sbq, sbq, R("sb_q"), sbn, MUL, MUL, "sbq_n")
            v.wait_ge(*after("sbk_rms"))
            link(v.reciprocal(sbn, sbn))
            stt(sbk, sbk, R("sb_k"), sbn, MUL, MUL, "sbk_n")
            cos, sin = (C(n).unsqueeze(1).broadcast_to([P, 2, T]) for n in ("cos", "sin"))
            for raw, out, bank, swap, name in ((rq, rqr, BO, "swap_q", "rot_q"), (rkk, rkr, BC, "swap_k", "rot_k")):
                tt(out, raw, cos, MUL)
                v.wait_ge(*after(swap))
                tt(scr, pair(bank), sin, MUL, name)
                tt(out, out, scr, ADD, name + "_in")
            v.wait_ge(*after("conv_b"))
            stt(u[:, :, PAD:PAD + T], acc, 1.0, u[:, :, PAD:PAD + T], ADD, MUL)

            def taps(first, last):
                for k in range(first, last):
                    for j in range(2):
                        w = R("dw", j * TAPS + k)
                        if k == 0:
                            ts(acc[:, j, :], u[:, j, 0:T], w, None, MUL)
                        else:
                            stt(acc[:, j, :], u[:, j, k:k + T], w, acc[:, j, :], MUL, ADD)

            for c in range(NCH):
                v.wait_ge(*after(f"p_gram_{c}"))
                tt(G[:, c], quad((Z0, Z1)[c % 2]), C("grams").rearrange("p (a n) -> p a n", a=4), MUL, f"gram_{c}")
                if c % 4 == 3:
                    g = c // 4
                    v.wait_ge(*after(f"p_A_{g}"))
                    A = M[:, 0] if g == 0 else A1
                    tt(A, quad(BX), C("negstrict").unsqueeze(1).broadcast_to([P, 4, P]), MUL, f"A_{g}")
                taps(4 * c, min(4 * c + 4, TAPS))

            def inverse_start(g):
                tt(TI[:, 4 * g:4 * g + 4, :], G[:, 4 * g:4 * g + 4, 0, :], ident.unsqueeze(1).broadcast_to([P, 4, P]), ADD,
                   f"TI_{g}_0")

            def mt_copy(g, k):
                v.wait_ge(*after(f"p_MT_{g}_{k}"))
                link(v.tensor_copy(MT[:, k % 2], quad(BX)), f"MT_{g}_{k}")

            def inverse_add(g, k):
                v.wait_ge(*after(f"p_TI_{g}_{k}"))
                t = TI[:, 4 * g:4 * g + 4, :]
                tt(t, t, quad(BY), ADD, f"TI_{g}_{k}")

            def ret_s(hh):
                z, out = (Z0, Z1)[hh % 2], (az, at_)[hh % 2]
                v.wait_ge(*after(f"p_ret_s_{hh}"))
                if hh >= 2:
                    v.wait_ge(*after(f"p_ret_o_{hh - 2}"))
                d = C("decay", hh * T, T)
                tt(out[:, 0:T], z[:, 0:T], d, MUL)
                tt(out[:, T:T + P], z[:, T:T + P], d[:, 0:P], MUL, f"ret_s_{hh}")

            inverse_start(0)
            inverse_start(1)
            ret_s(0)
            mt_copy(0, 1)
            for k in range(1, 5):
                inverse_add(0, k)
                if k < 3:
                    mt_copy(0, k + 1)
                if k < 4:
                    ret_s(k)
            for j in range(2):
                ts(acc[:, j, :], acc[:, j, :], 0.5, R("conv_b", j), MUL, ADD, name="conv_y" if j else None)
            mt_copy(1, 1)
            v.wait_ge(*after("ret_sum"))
            stt(rkk, pair(Z0), -1.0 / HD, rq, MUL, ADD, "ret_xc")
            inverse_add(1, 1)
            mt_copy(1, 2)
            v.wait_ge(*after("ret_std"))
            link(v.reciprocal(rq, rq))
            for j in range(2):
                stt(rkk[:, j, :], rkk[:, j, :], R("ret_gn", j), rq[:, j, :], MUL, MUL)
            tt(rg, rg, rkk, MUL, "ret_out")
            inverse_add(1, 2)
            mt_copy(1, 3)
            v.wait_ge(*after("conv_sum"))
            for j in range(2):
                stt(acc[:, j, :], Z0[:, 0:T], -1.0 / T, acc[:, j, :], MUL, ADD, "conv_xc" if j else None)
            inverse_add(1, 3)
            v.wait_ge(*after("conv_std"))
            link(v.reciprocal(at_[:, 0:T], at_[:, 0:T]))
            for j in range(2):
                stt(acc[:, j, :], acc[:, j, :], R("conv_ln_w", j), at_[:, 0:T], MUL, MUL)
            for j in range(2):
                ts(acc[:, j, :], acc[:, j, :], R("conv_ln_b", j), None, ADD, name="conv_lin" if j else None)
            v.wait_ge(*after("conv_th"))
            ts(scr, scr, 0.5, 0.5, MUL, ADD)
            tt(acc, acc, scr, MUL, "conv_out")
            inverse_add(1, 4)

            def apply(branch, slot, banks2):
                for q in range(4):
                    v.wait_ge(*after(f"p_{branch}_{q}"))
                    bank = pair(banks2[q % 2])
                    gt = gates[:, slot, 2 * q:2 * q + 2, :]
                    out = merged[:, 2 * q:2 * q + 2, :]
                    if branch == "conv":
                        stt(out, gt, 1.0, bank, ADD, MUL, f"applied_{branch}_{q}")
                    else:
                        stt(scr, gt, 1.0, bank, ADD, MUL, f"applied_{branch}_{q}")
                        tt(out, out, scr, ADD, "merged" if (branch, q) == ("rw", 3) else None)

            apply("conv", 0, (P1, P0))
            apply("ret", 1, (P1, P0))

            for c in range(NCH):
                hh = c // 2
                v.wait_ge(*after(f"p_rhs_{c}"))
                ts(rhsn, BC[:, 0:HD], -1.0, None, MUL, name=f"rhs_{c}")
                if c and c < NCH - 1:
                    for j in range(2):
                        ts(Se[:, j, :], S[:, c % 2, j, :], dec[:, j, c:c + 1], None, MUL)
                if c % 2 == 0:
                    z = (Z0, Z1)[hh % 2][:, 0:384]
                    v.wait_ge(*after(f"sb_z_{hh}"))
                v.wait_ge(*after(f"p_sa_{c}"))
                link(v.tensor_copy(sa, BC[:, HD:2 * HD]), f"sa_{c}")
                if c % 2 == 0:
                    v.wait_ge(*after(f"sb_ln_{hh}"))
                    stt(az, z, 0.0, exz, MAX, ADD, f"sb_sp_{hh}_raw")
                    for o in (0, T):
                        tt(az[:, o:o + P], az[:, o:o + P], C("strictT"), MUL, f"sb_sp_{hh}" if o else None)
                if c < NCH - 1:
                    v.wait_ge(*after(f"p_S_{c + 1}"))
                    for j in range(2):
                        o = BC[:, (2 + j) * HD:(3 + j) * HD]
                        d = dec[:, j, c:c + 1]
                        if c == 0:
                            ts(S[:, 1, j, :], o, d, None, MUL, name="S_1" if j else None)
                        else:
                            stt(S[:, (c + 1) % 2, j, :], o, d, Se[:, j, :], MUL, ADD, f"S_{c + 1}" if j else None)
            v.wait_ge(*after("p_y_7"))
            link(v.tensor_copy(yst, BY.rearrange("p (c v) -> p c v", c=NCH)), "y")
            link(v.tensor_reduce(small[:, 0:8], yst, AX.X, ADD))
            ts(small[:, 0:8], small[:, 0:8], 1.0 / HD, None, MUL)
            tt(yst, yst, small[:, 0:8].unsqueeze(2).broadcast_to([P, NCH, HD]), SUB)
            tt(ysq, yst, yst, MUL)
            link(v.tensor_reduce(small[:, 0:8], ysq, AX.X, ADD), "y_var")
            v.wait_ge(*after("y_std"))
            link(v.reciprocal(small[:, 8:16], small[:, 8:16]))
            tt(yst, yst, small[:, 8:16].unsqueeze(2).broadcast_to([P, NCH, HD]), MUL, "yn")
            apply("sb", 0, (P1, P0))
            for a in range(2):
                v.wait_ge(*after(f"p_yT_{a}"))
                for hh in range(4):
                    src = (Z0, Z1)[a][0:HD, :].rearrange("p (c n) -> p c n", c=4)[:, :, hh * CH:(hh + 1) * CH]
                    dst = yT[(hh % 2) * HD:(hh % 2 + 1) * HD, hh // 2, a * P:(a + 1) * P].rearrange("p (c t) -> p c t", c=4)
                    link(v.tensor_copy(dst, src), f"yT_{a}" if hh == 3 else None)
            for j in range(2):
                ts(yT[:, j, :], yT[:, j, :], R("rw_ln_w", j), R("rw_ln_b", j), MUL, ADD)
            tt(yT, yT, bonus, ADD)
            tt(gg, gg, yT, MUL, "rw_out")
            apply("rw", 1, (P1, P0))
            for q in range(4):
                v.wait_ge(*after(f"p_x_{q}"))
                xs = x[:, 2 * q:2 * q + 2, :]
                stt(xs, pair((P1, P0)[q % 2]), 0.5, xs, MUL, ADD, ("all_read" if q == 3 else f"x_{q}"))
    phase_end(env)


def ffn_phase(env, layer):
    nc, x, h, banks = env["nc"], env["x"], env["h"], env["banks"]
    after, done, C, eps, ident, col, plan = (env[n] for n in ("after", "done", "C", "eps", "ident", "col", "plan"))
    n_parts = nc.snap(layer * (EXPERTS - DENSE_PARTS) + DENSE_PARTS)
    first_round = nc.snap(layer * LAYER0_ROUNDS + MIX_ROUNDS)
    hid_banks = [banks[n] for n in ("P0", "P1", "Z0")]
    out_banks = [banks[n] for n in ("O", "C", "Y", "X")]
    BZ = banks["Z1"]
    FREE = len(hid_banks)
    tiles_in = env["sem"]("hidden_tiles_in_psum")
    gated = env["sem"]("hidden_tiles_silu")
    hid_done = env["sem"]("hidden_tiles_done_and_banks_free")
    y_done = env["sem"]("hidden_tiles_multiplied")
    tmp_written = env["sem"]("hidden_products_written")

    cut = carver(env)
    prm = cut(PN)
    R = lambda name, i=0, n=1: col(prm, PCOL, name, i, n)
    sqx = cut(KD, T)
    rms = cut(T)
    lg, lg2, wt = cut(2, 8), cut(2, 8), cut(2, 8)
    m1, m2 = cut(2, 8), cut(2, 8)
    i1 = cut(2, 8)
    i2 = cut(2, 8)
    i1u, i2u = i1.bitcast(U32), i2.bitcast(U32)
    idx = cut(2, 2)
    oh1, oh2 = cut(2, 8), cut(2, 8)
    dm, g12 = cut(2), cut(2, 2)
    wT = cut(T)
    wb = cut(EXPERTS, T)
    sl, hid, tmp = cut(3, T), cut(3, T), cut(T)

    with nc.Block() as block:
        @block.sync
        def _(sp):
            load_rounds(env, sp, sp.snap(first_round + 1), sp.snap(n_parts * EXP_ROUNDS))

        @block.tensor
        def _(pe):
            pe.wait_ge(*after("sqx"))
            for k in range(KD):
                mm = pe.matmul(BZ[:, 0:T], C("ones"), sqx[:, k, :], start=(k == 0), stop=(k == KD - 1))
            mm.then_inc(*done("pe", "ssx"))
            pe.wait_ge(*after("h"))
            router = R("router", 0, 64).rearrange("p (k e) -> p k e", k=KD)
            for a in range(TT2):
                for k in range(KD):
                    mm = pe.matmul(BZ[:, a * 8:a * 8 + 8], h[:, k, a * P:(a + 1) * P], router[:, k, :], start=(k == 0),
                                   stop=(k == KD - 1))
            mm.then_inc(*done("pe", "logits"))
            pe.wait_ge(*after("weights"))
            for a in range(TT2):
                mm = pe.transpose(BZ[0:8, a * P:(a + 1) * P], wt[:, a, :], ident)
            mm.then_inc(*done("pe", "wT"))
            pe.wait_ge(*after("wT_copy"))
            for e in range(EXPERTS):
                pe.wait_ge(*after(f"wb_{e - 1}" if e else "wT_copy"))
                pe.matmul(BZ[:, 0:T], ident[0:8, e:e + 1].broadcast_to([8, P]), wT[0:8, :], start=True, stop=True)\
                  .then_inc(*done("pe", f"spread_{e}"))
            pe.wait_ge(*after("zero_out"))
            with pe.Fori(0, n_parts) as e:
                blocks = Blocks(env, pe, pe.snap(first_round + e * EXP_ROUNDS))

                def down(f):
                    w2 = blocks.next()
                    pe.wait_ge(hid_done, pe.snap(e * FF_TILES + (FREE + f + 1)))
                    for d in range(KD):
                        mm = pe.matmul(out_banks[d // 2][:, (d % 2) * T:(d % 2 + 1) * T], w2[:, d * P:(d + 1) * P],
                                       hid[:, f % 3, :], start=False, stop=False, skip_group_check=True)
                        if d == 0:
                            blocks.release(mm)
                    mm.then_inc(y_done, 1)
                    blocks.unreleased += 1

                for f in range(FF_TILES):
                    bank = hid_banks[f % 3]
                    pe.wait_ge(hid_done, pe.snap(e * FF_TILES + (f + 2 if f < 2 else f + 1)))
                    for i in range(2):
                        w = blocks.col()
                        for k in range(KD):
                            mm = pe.matmul(bank[:, i * T:(i + 1) * T], w[:, k, :], h[:, k, :], start=(k == 0),
                                           stop=(k == KD - 1))
                            if k == 0:
                                blocks.release(mm)
                        blocks.unreleased += 1
                    mm.then_inc(tiles_in, 1)
                    if f:
                        down(f - 1)
                down(FF_TILES - 1)
                blocks.release(pe.matmul(BZ[0:1, 0:1], ident[0:1, 0:1], ident[0:1, 0:1], start=True, stop=True))

        @block.scalar
        def _(a):
            a.activation(sqx, x, ACT.Square).then_inc(*done("act", "sqx"))
            a.wait_ge(*after("ssx"))
            a.activation(rms, BZ[:, 0:T], ACT.Sqrt, scale=1.0 / D, bias=eps("norm")).then_inc(*done("act", "x_rms"))
            a.wait_ge(*after("gate_diff"))
            a.activation(dm, dm, ACT.Exp).then_inc(*done("act", "gate_exp"))
            with a.Fori(0, n_parts) as e:
                for f in range(FF_TILES):
                    a.wait_ge(tiles_in, a.snap(e * FF_TILES + (f + 1)))
                    a.activation(sl[:, f % 3, :], hid_banks[f % 3][:, 0:T], ACT.Silu).then_inc(gated, 1)

        @block.vector
        def _(v):
            def link(ins, name=None):
                ins.then_inc(*done("dve", name))
                v.wait_ge(plan.sem["dve"], plan.count["dve"])

            for b in out_banks:
                link(v.memset(b, 0.0), "zero_out" if b is out_banks[-1] else None)
            v.wait_ge(*after("x_rms"))
            link(v.reciprocal(rms, rms))
            for k in range(KD):
                link(v.scalar_tensor_tensor(out=h[:, k, :], in0=x[:, k, :], scalar=R("norm_ffn", k), in1=rms,
                                            op0=ALU.mult, op1=ALU.mult), "h" if k == KD - 1 else None)
            v.wait_ge(*after("logits"))
            link(v.tensor_copy(lg, BZ[:, 0:16].rearrange("p (a e) -> p a e", a=2)), "logits_copy")
            iota = C("iota8")
            for a in range(TT2):
                link(v.max(m1[:, a, :], lg[:, a, :]))
                link(v.max_index(i1u[:, a, :], m1[:, a, :], lg[:, a, :]))
                link(v.tensor_copy(idx[:, a, 0:1], i1u[:, a, 0:1]))
                link(v.tensor_scalar(oh1[:, a, :], iota, idx[:, a, 0:1], None, ALU.is_equal))
                link(v.scalar_tensor_tensor(out=lg2[:, a, :], in0=oh1[:, a, :], scalar=NEG, in1=lg[:, a, :],
                                            op0=ALU.mult, op1=ALU.add))
                link(v.max(m2[:, a, :], lg2[:, a, :]))
                link(v.max_index(i2u[:, a, :], m2[:, a, :], lg2[:, a, :]))
                link(v.tensor_copy(idx[:, a, 1:2], i2u[:, a, 0:1]))
                link(v.tensor_scalar(oh2[:, a, :], iota, idx[:, a, 1:2], None, ALU.is_equal))
                link(v.tensor_tensor(dm[:, a:a + 1], m2[:, a, 0:1], m1[:, a, 0:1], ALU.subtract), "gate_diff" if a else None)
            v.wait_ge(*after("gate_exp"))
            link(v.tensor_scalar(g12[:, 0, :], dm, 1.0, None, ALU.add))
            link(v.reciprocal(g12[:, 0, :], g12[:, 0, :]))
            link(v.tensor_tensor(g12[:, 1, :], g12[:, 0, :], dm, ALU.mult))
            for a in range(TT2):
                link(v.tensor_scalar(wt[:, a, :], oh1[:, a, :], g12[:, 0, a:a + 1], None, ALU.mult))
                link(v.scalar_tensor_tensor(out=wt[:, a, :], in0=oh2[:, a, :], scalar=g12[:, 1, a:a + 1],
                                            in1=wt[:, a, :], op0=ALU.mult, op1=ALU.add))
                link(v.tensor_scalar(wt[:, a, :], wt[:, a, :], R("is_moe"), R("is_dense"), ALU.mult, ALU.add),
                     "weights" if a else None)
            v.wait_ge(*after("wT"))
            link(v.tensor_copy(wT[0:8, :], BZ[0:8, 0:T]), "wT_copy")
            for e in range(EXPERTS):
                v.wait_ge(*after(f"spread_{e}"))
                link(v.tensor_copy(wb[:, e, :], BZ[:, 0:T]), f"wb_{e}")
            v.memset(tmp, 0.0).then_inc(hid_done, FREE)
            v.wait_ge(hid_done, FREE)
            with v.Fori(0, n_parts) as e:
                for f in range(FF_TILES):
                    v.wait_ge(gated, v.snap(e * FF_TILES + (f + 1)))
                    v.wait_ge(hid_done, v.snap(e * FF_TILES + (FREE + f)))
                    v.tensor_tensor(tmp, sl[:, f % 3, :], hid_banks[f % 3][:, T:2 * T], ALU.mult).then_inc(tmp_written, 1)
                    v.wait_ge(tmp_written, v.snap(e * FF_TILES + (f + 1)))
                    if f >= 3:
                        v.wait_ge(y_done, v.snap(e * FF_TILES + (f - 2)))
                    v.tensor_tensor(hid[:, f % 3, :], tmp, wb[:, e, :], ALU.mult).then_inc(hid_done, 1)
                v.wait_ge(y_done, v.snap((e + 1) * FF_TILES))
            for q in range(4):
                xs = x[:, 2 * q:2 * q + 2, :]
                link(v.tensor_tensor(xs, xs, out_banks[q].rearrange("p (j t) -> p j t", j=2), ALU.add))
    phase_end(env)


def second_phase(env):
    nc, dram, x, h, banks = env["nc"], env["dram"], env["x"], env["h"], env["banks"]
    after, done, C, eps, ident, col, plan = (env[n] for n in ("after", "done", "C", "eps", "ident", "col", "plan"))
    P0, P1, Z0, Z1, BO, BC, BY, BX = (banks[n] for n in ("P0", "P1", "Z0", "Z1", "O", "C", "Y", "X"))
    pair = lambda b: b.rearrange("p (j t) -> p j t", j=2)
    cut = carver(env)
    prm = cut(QN)
    R = lambda name, i=0, n=1: col(prm, QCOL, name, i, n)
    sqx = cut(KD, T)
    rms = cut(T)
    q = cut(4, T)
    kk = cut(2, T)
    vals = cut(2, TT2, P)
    kv2, kvv = cut(2, T), cut(2, T)
    blk = cut(16, 2, NC)
    hid = cut(2, 2, 2, NC)
    hidf = cut(2, 2 * NC)
    kc, vc = cut(NC + 1), cut(P)
    brg = cut(2, 24)
    tabs = cut(8, 384)
    ctab = cut(8, T)
    cbias = cut(16, NC)
    sc = cut(16, NC)
    st = cut(16)
    st2 = cut(16)
    pcT = cut(8, T)
    vec = cut(2, 512)
    prob = [cut(384) for _ in range(2)]
    probT = [cut(384) for _ in range(2)]
    mx, sums, fac = cut(32), cut(32), cut(32)
    o = cut(4, T)
    gn = cut(4, T)
    uc, ru, iu, gl = cut(4, T), cut(4, T), cut(4, T), cut(4, T)
    up = cut(4, 3 + T)
    sp8 = cut(40)
    mg = cut(KD, T)
    mga = cut(KD, T)
    tmp, lrec = cut(4, T), cut(4, T)
    ysb = tabs.rearrange("p h n -> p (h n)")[:, 0:TT2 * D].rearrange("p (a n) -> p a n", a=TT2)
    first = SEC_FIRST_ROUND
    vec_dram = dram["bias_vec"]

    with nc.Block() as block:
        @block.sync
        def _(sp):
            sp.wait_ge(*after("vec"))
            sp.dma_start(vec_dram.rearrange("(i h) n -> h i n", i=2), vec[0:8]).then_inc(*done("par", "vec_out", by=16))
            sp.wait_ge(*after("vec_out"))
            for a, (at, n) in enumerate(((0, P), (P, T))):
                for hh in range(8):
                    src = bass.AP(vec_dram.tensor, hh * 512 + (P if a == 0 else 0), [[1, P], [1, n]])
                    sp.dma_start(tabs[:, hh, at:at + n], src).then_inc(*done("par", by=16))
            src = bass.AP(vec_dram.tensor, 8 * 512, [[16, NC], [512, 8], [1, T]])
            sp.dma_start(ctab[0:NC], src).then_inc(*done("par", "tables", by=16))
            load_rounds(env, sp, first + 1, SEC_ROUNDS - 1)
            for a in range(TT2):
                sp.wait_ge(*after(f"yh_{a}_1"))
                sp.dma_start(dram["out"].rearrange("o (a p) d -> a p (o d)", p=P)[a], ysb[:, a, :])\
                  .then_inc(*done("par", "stored", by=16) if a else done("par", by=16))
            sp.wait_ge(*after("stored"))

        @block.gpsimd
        def _(g):
            g.memset(up[:, :, 0:3], 0.0).then_inc(*done("pool", "zeroed"))

        @block.tensor
        def _(pe):
            blocks = Blocks(env, pe, first)
            turn, readers = [0], {}

            def take(bank, reader):
                if bank.tensor.name in readers:
                    pe.wait_ge(*after(readers[bank.tensor.name]))
                readers[bank.tensor.name] = reader

            pe.wait_ge(env["sem"]("params2_in"), 16)
            for i in range(2):
                take((BC, BY)[i], "vec")
                mm = pe.matmul((BC, BY)[i][0:8, 0:VEC], R("rel", 0, 8)[0:BUCKETS + 1, :],
                               R("onehot", i * VEC, VEC)[0:BUCKETS + 1, :], start=True, stop=True)
            mm.then_inc(*done("pe", "p_vec"))
            pe.wait_ge(*after("sqx"))
            take(BX, "x_rms")
            for k in range(KD):
                mm = pe.matmul(BX[:, 0:T], C("ones"), sqx[:, k, :], start=(k == 0), stop=(k == KD - 1))
            mm.then_inc(*done("pe", "ssx"))
            pe.wait_ge(*after("h"))

            def tile(bank, j, src=None, rows=KD):
                src = h if src is None else src
                w = blocks.col()
                for k in range(rows):
                    mm = pe.matmul(bank[:, j * T:(j + 1) * T], w[:, k, :], src[:, k, :], start=(k == 0), stop=(k == rows - 1))
                    if k == 0:
                        blocks.release(mm)
                blocks.unreleased += 1
                return mm

            def tile_tm(bank, j):
                w = blocks.col()
                for a in range(TT2):
                    for k in range(KD):
                        mm = pe.matmul(bank[:, j * T + a * P:j * T + (a + 1) * P], h[:, k, a * P:(a + 1) * P], w[:, k, :],
                                       start=(k == 0), stop=(k == KD - 1))
                        if k == 0 and a == 0:
                            blocks.release(mm)
                blocks.unreleased += 1
                return mm

            def big(name, reader, fs):
                bank = (P0, P1)[turn[0] % 2]
                turn[0] += 1
                take(bank, reader)
                for j, f in enumerate(fs):
                    mm = f(bank, j)
                mm.then_inc(*done("pe", name))

            big("p_kvc", "vc_raw", (tile, tile))
            big("p_q0", "q0", (tile, tile))
            big("p_q1", "q1", (tile, tile))
            big("p_k", "k_raw", (tile, tile))
            big("p_v", "v_tm", (tile_tm, tile_tm))
            take(BY, "brg")
            br = R("br", 0, 192).rearrange("p (k n) -> p k n", k=KD)
            for a in range(TT2):
                for k in range(KD):
                    mm = pe.matmul(BY[:, a * 24:(a + 1) * 24], h[:, k, a * P:(a + 1) * P], br[:, k, :], start=(k == 0),
                                   stop=(k == KD - 1))
            mm.then_inc(*done("pe", "p_br"))
            for j, (src, name) in enumerate(((0, "q0"), (1, "q1"))):
                take((Z0, Z1)[j], f"{name}_rms")
                pe.wait_ge(*after(f"{name}_sq"))
                pe.matmul((Z0, Z1)[j], C("headones"), sqx[:, 2 * j:2 * j + 2, :].rearrange("p j t -> p (j t)"), start=True,
                          stop=True).then_inc(*done("pe", f"{name}_ss"))
            take(BX, "k_rms")
            pe.wait_ge(*after("k_sq"))
            pe.matmul(BX, C("headones"), sqx[:, 4:6, :].rearrange("p j t -> p (j t)"), start=True, stop=True)\
              .then_inc(*done("pe", "k_ss"))
            for i, name in enumerate(("k", "v")):
                bank = (BC, BO)[i]
                take(bank, f"hid_{name}")
                pe.wait_ge(*after(f"blk_{name}"))
                for b in range(4):
                    w = blocks.next().rearrange("p (n o) -> p n o", n=4)
                    for n in range(4):
                        for half in range(2):
                            mm = pe.matmul(bank[:, half * 2 * NC:(half + 1) * 2 * NC], w[:, n, half * P:(half + 1) * P],
                                           blk[:, 4 * b + n].rearrange("p g c -> p (g c)"), start=(b, n, half) == (0, 0, 0),
                                           stop=(b, n) == (3, 3), skip_group_check=True)
                            if (n, half) == (0, 0):
                                blocks.release(mm)
                    blocks.unreleased += 1
                mm.then_inc(*done("pe", f"p_hid_{name}"))
                big(f"p_gn{i}", f"gn{i}", (tile, tile))
            w2 = R("w2", 0, 256).rearrange("p (i u d) -> p i u d", i=2, u=2)
            take(BY, "kc_raw")
            pe.wait_ge(*after("hid_k"))
            for g in range(2):
                for half in range(2):
                    mm = pe.matmul(BY[g * HD:(g + 1) * HD, 0:NC], w2[:, 0, half, :], hid[:, 0, half, g, :], start=(half == 0),
                                   stop=(half == 1))
            mm.then_inc(*done("pe", "p_kc"))
            big("p_u0", "u0", (tile, tile))
            take(BC, "vc")
            pe.wait_ge(*after("hid_v"))
            for g in range(2):
                for half in range(2):
                    mm = pe.matmul(BC[0:NC, g * HD:(g + 1) * HD], hid[:, 1, half, g, :], w2[:, 1, half, :], start=(half == 0),
                                   stop=(half == 1))
            mm.then_inc(*done("pe", "p_vc"))
            take(BY, "kc_rms")
            pe.wait_ge(*after("kc_sq"))
            pe.matmul(BY[:, 0:NC], C("headones"), rms[:, 0:NC], start=True, stop=True).then_inc(*done("pe", "kc_ss"))
            big("p_u1", "u1", (tile, tile))
            pe.wait_ge(*after("tables"))
            for b in range(2):
                take((Z0, Z1)[b], f"cbias_{b}")
                for i in range(8):
                    hh = b * 4 + i // 2
                    mm = pe.matmul((Z0, Z1)[b][:, i * NC:(i + 1) * NC], ctab[0:NC, hh, (i % 2) * P:(i % 2 + 1) * P],
                                   C("flip")[0:NC, P - NC:P], start=True, stop=True)
                mm.then_inc(*done("pe", f"p_cbias_{b}"))
            pe.wait_ge(*after("kc"))
            pe.wait_ge(*after("q1_n"))
            for b in range(2):
                take((BY, BX)[b], f"csc_{b}")
                for i in range(8):
                    j, a = i // 2, i % 2
                    mm = pe.matmul((BY, BX)[b][:, i * NC:(i + 1) * NC], q[b * HD:(b + 1) * HD, j, a * P:(a + 1) * P],
                                   kc[b * HD:(b + 1) * HD, 0:NC], start=True, stop=True)
                mm.then_inc(*done("pe", f"p_csc_{b}"))
            big("p_gl0", "gl0", (tile, tile))
            wa, wx = (R(n, 0, 512).rearrange("p (j n) -> p j n", j=4) for n in ("wa", "wx"))
            for i, (w, n) in enumerate(((wa, "r"), (wx, "i"))):
                for half in range(2):
                    bank = (Z0, Z1)[half]
                    take(bank, f"lru_{n}{half}")
                    pe.wait_ge(*after(f"uc{half}"))
                    for j in range(2):
                        mm = pe.matmul(bank[:, j * T:(j + 1) * T], w[:, 2 * half + j, :], uc[:, 2 * half + j, :], start=True,
                                       stop=True)
                    mm.then_inc(*done("pe", f"p_lru_{n}{half}"))
            big("p_gl1", "gl1", (tile, tile))
            pe.wait_ge(*after("cprob"))
            for b in range(4):
                bank = (BC, BO, BY, BX)[b]
                take(bank, f"pcT_{b}")
                for i in range(4):
                    mm = pe.transpose(bank[0:NC, i * P:(i + 1) * P], sc[:, 4 * b + i, :], ident)
                mm.then_inc(*done("pe", f"p_pcT_{b}"))

            def scores(n):
                hn, br_ = n // 2, n % 2
                j, b = hn // 2, hn % 2
                bank = (Z0, Z1)[n % 2]
                take(bank, f"exp_{n}")
                pe.matmul(bank[:, 0:P], q[b * HD:(b + 1) * HD, j, 0:P], kk[b * HD:(b + 1) * HD, br_, 0:P], start=True,
                          stop=False, skip_group_check=True)
                pe.matmul(bank[:, P:P + T], q[b * HD:(b + 1) * HD, j, P:T], kk[b * HD:(b + 1) * HD, br_, :], start=False,
                          stop=False, skip_group_check=True)
                pe.matmul(bank[:, 0:P + T], C("flip"), tabs[:, j + 4 * b, :], start=False, stop=True,
                          skip_group_check=True).then_inc(*done("pe", f"p_scores_{n}"))

            def turn_probs(n):
                pe.wait_ge(*after(f"prob_{n}"))
                bank = (BC, BY)[n % 2]
                take(bank, f"probT_{n}")
                pr = prob[n % 2]
                pe.transpose(bank[:, 0:P], pr[:, 0:P], ident)
                pe.transpose(bank[:, P:T], pr[:, P:T], ident)
                pe.transpose(bank[:, T:T + P], pr[:, T:T + P], ident).then_inc(*done("pe", f"p_probT_{n}"))

            def gather(n):
                hn, br_ = n // 2, n % 2
                j, b = hn // 2, hn % 2
                bank = (BO, BX)[j // 2]
                if n == 0 or n == 8:
                    take(bank, f"o_{n // 8}")
                out = bank[b * HD:(b + 1) * HD, (j % 2) * T:(j % 2 + 1) * T]
                late = bank[b * HD:(b + 1) * HD, (j % 2) * T + P:(j % 2 + 1) * T]
                pe.wait_ge(*after(f"probT_{n}"))
                if br_ == 0:
                    pe.matmul(out, vc[0:NC, b * HD:(b + 1) * HD], pcT[0:NC, j + 4 * b, :], start=True, stop=False,
                              skip_group_check=True)
                pT = probT[n % 2]
                pe.matmul(out, vals[:, br_, 0, b * HD:(b + 1) * HD], pT[:, 0:T], start=False, stop=False,
                          skip_group_check=True)
                mm = pe.matmul(late, vals[:, br_, 1, b * HD:(b + 1) * HD], pT[:, T:T + P], start=False, stop=(br_ == 1),
                               skip_group_check=True)
                mm.then_inc(*done("pe", f"p_o_{n}"))

            scores(0)
            scores(1)
            pe.wait_ge(*after("pcT_3"))
            for n in range(16):
                if n % 2 == 0:
                    mbank = (P0, P1)[turn[0] % 2]
                    take(mbank, f"mg_{n // 2}")
                mm = tile(mbank, n % 2)
                if n % 2:
                    mm.then_inc(*done("pe", f"p_mg_{n // 2}"))
                    turn[0] += 1
                turn_probs(n)
                if n + 2 < 16:
                    scores(n + 2)
                if n:
                    gather(n - 1)
            gather(15)

            def rows(name, src, ready):
                pe.wait_ge(*after(ready))
                w = [blocks.next() for _ in range(4)]
                for i in range(4):
                    bank = (P0, P1)[turn[0] % 2]
                    turn[0] += 1
                    take(bank, f"{name}_{i}")
                    for j in range(2):
                        for c in range(4):
                            mm = pe.matmul(bank[:, j * T:(j + 1) * T], w[c][:, (2 * i + j) * P:(2 * i + j + 1) * P],
                                           src[:, c, :], start=(c == 0), stop=(c == 3))
                            if c == 0:
                                blocks.release(mm)
                    mm.then_inc(*done("pe", f"p_{name}_{i}"))
                blocks.unreleased += 4

            rows("yb", gl, "lru")
            rows("ya", o, "o_1")
            pe.wait_ge(*after("merged"))
            for i in range(4):
                big(f"p_x_{i}", f"x_{i}", (lambda b, j: tile(b, j, src=sqx),) * 2)
            for a in range(TT2):
                for g in range(2):
                    bank = (Z0, Z1)[g]
                    take(bank, f"yh_{a}_{g}")
                    pe.wait_ge(*after("x_3"))
                    for i in range(4):
                        mm = pe.transpose(bank[:, i * P:(i + 1) * P], x[:, 4 * g + i, a * P:(a + 1) * P], ident)
                    mm.then_inc(*done("pe", f"p_y_{a}_{g}"))
            for _ in range(SEC_BLOCKS - blocks.n):
                blocks.next()

        @block.scalar
        def _(a):
            def link(ins, name=None):
                ins.then_inc(*done("act", name))
                a.wait_ge(plan.sem["act"], plan.count["act"])

            def act(out, in_, func, name=None, **kw):
                link(a.activation(out, in_, func, **kw), name)

            a.dma_start(prm, dram["params2"]).then_inc(env["sem"]("params2_in"), 16)
            act(sqx, x, ACT.Square, "sqx")
            a.wait_ge(*after("ssx"))
            act(rms, BX[:, 0:T], ACT.Sqrt, "x_rms", scale=1.0 / D, bias=eps("norm"))
            a.wait_ge(*after("p_q0"))
            act(q[:, 0:2, :], pair(P1), ACT.Copy, "q0")
            act(sqx[:, 0:2, :], q[:, 0:2, :], ACT.Square, "q0_sq")
            a.wait_ge(*after("p_q1"))
            act(q[:, 2:4, :], pair(P0), ACT.Copy, "q1")
            act(sqx[:, 2:4, :], q[:, 2:4, :], ACT.Square, "q1_sq")
            a.wait_ge(*after("p_k"))
            act(kk, pair(P1), ACT.Copy, "k_raw")
            act(sqx[:, 4:6, :], kk, ACT.Square, "k_sq")
            a.wait_ge(*after("p_v"))
            act(vals.rearrange("p i a n -> p i (a n)"), pair(P0), ACT.Copy, "v_tm")
            for j in range(2):
                a.wait_ge(*after(f"q{j}_ss"))
                act(tmp[:, 2 * j:2 * j + 2, :], pair((Z0, Z1)[j]), ACT.Sqrt, f"q{j}_rms", bias=eps("sbq"))
            a.wait_ge(*after("k_ss"))
            act(mg[:, 0:2, :], pair(BX), ACT.Sqrt, "k_rms", scale=1.0 / HD, bias=eps("norm"))
            a.wait_ge(*after("p_br"))
            act(brg.rearrange("p a n -> p (a n)"), BY[:, 0:48], ACT.Sigmoid, "brg")
            for i, name in enumerate(("k", "v")):
                a.wait_ge(*after(f"p_hid_{name}"))
                for half in range(2):
                    act(hid[:, i, half].rearrange("p g c -> p (g c)"), (BC, BO)[i][:, half * 2 * NC:(half + 1) * 2 * NC],
                        ACT.Silu, f"hid_{name}" if half else None, bias=R("b1", 2 * i + half))
                a.wait_ge(*after(f"p_gn{i}"))
                act(gn[:, 2 * i:2 * i + 2, :], pair((P1, P0)[i]), ACT.Silu, f"gn{i}")
            a.wait_ge(*after("p_kc"))
            act(kc[:, 0:NC], BY[:, 0:NC], ACT.Copy, "kc_raw")
            act(rms[:, 0:NC], kc[:, 0:NC], ACT.Square, "kc_sq")
            a.wait_ge(*after("zeroed"))
            a.wait_ge(*after("p_u0"))
            act(up[:, 0:2, 3:3 + T], pair(P1), ACT.Copy, "u0")
            a.wait_ge(*after("p_vc"))
            act(vc[0:NC, :], BC[0:NC, 0:P], ACT.Copy, "vc")
            a.wait_ge(*after("kc_ss"))
            act(rms[:, 16:16 + NC], BY[:, 0:NC], ACT.Sqrt, "kc_rms", scale=1.0 / HD, bias=eps("norm"))
            a.wait_ge(*after("p_u1"))
            act(up[:, 2:4, 3:3 + T], pair(P0), ACT.Copy, "u1")
            a.wait_ge(*after("lam_abs"))
            act(sp8[:, 4:8], sp8[:, 0:4], ACT.Exp, "lam_exp", scale=-1.0)
            a.wait_ge(*after("csub"))
            act(sc, sc, ACT.Exp, "cexp")
            a.wait_ge(*after("p_gl0"))
            act(gl[:, 0:2, :], pair(P1), ACT.Silu, "gl0")
            for n, out, bias in (("r", ru, "ba"), ("i", iu, "bx")):
                for half in range(2):
                    a.wait_ge(*after(f"p_lru_{n}{half}"))
                    for j in range(2):
                        act(out[:, 2 * half + j, :], (Z0, Z1)[half][:, j * T:(j + 1) * T], ACT.Sigmoid,
                            f"lru_{n}{half}" if j else None, bias=R(bias, 2 * half + j))
            a.wait_ge(*after("p_gl1"))
            act(gl[:, 2:4, :], pair(P0), ACT.Silu, "gl1")
            a.wait_ge(*after("lam"))
            for j in range(4):
                act(ru[:, j, :], ru[:, j, :], ACT.Tanh, "lru_th" if j == 3 else None, scale=sp8[:, 36 + j:37 + j])
            act(tmp, ru, ACT.Sqrt, "lru_sqrt", scale=-1.0)

            for n in range(16):
                a.wait_ge(*after(f"shift_{n}"))
                if n >= 2:
                    a.wait_ge(*after(f"p_probT_{n - 2}"))
                pr = prob[n % 2]
                for i, (o0, w) in enumerate(((0, P), (P, T))):
                    c = 2 * n + i
                    act(pr[:, o0:o0 + w], (Z0, Z1)[n % 2][:, o0:o0 + w], ACT.Exp, f"exp_{n}" if i else None, bias=mx[:, c:c + 1],
                        accum_out=sums[:, c:c + 1])
                if n:
                    a.wait_ge(*after(f"p_probT_{n - 1}"))
                    if n >= 3:
                        a.wait_ge(*after(f"p_o_{n - 3}"))
                    act(probT[(n - 1) % 2], (BC, BY)[(n - 1) % 2][:, 0:384], ACT.Copy, f"probT_{n - 1}")
                if n % 2:
                    i = n // 2
                    a.wait_ge(*after(f"p_mg_{i}"))
                    out = mg[:, 2 * i:2 * i + 2, :] if i < 4 else mga[:, 2 * (i - 4):2 * (i - 4) + 2, :]
                    act(out, pair((P1, P0)[i % 2]), ACT.Tanh, f"mg_{i}", scale=0.5)
            a.wait_ge(*after("p_probT_15"))
            act(probT[1], BY[:, 0:384], ACT.Copy, "probT_15")

        @block.vector
        def _(v):
            def link(ins, name=None):
                ins.then_inc(*done("dve", name))
                v.wait_ge(plan.sem["dve"], plan.count["dve"])

            tt = lambda out, a0, a1, op, name=None: link(v.tensor_tensor(out, a0, a1, op), name)
            ts = lambda out, a0, s1, s2, op0, op1=None, name=None: link(
                v.tensor_scalar(out, a0, s1, s2, op0) if op1 is None else v.tensor_scalar(out, a0, s1, s2, op0, op1), name)
            stt = lambda out, a0, s, a1, op0, op1, name=None: link(
                v.scalar_tensor_tensor(out=out, in0=a0, scalar=s, in1=a1, op0=op0, op1=op1), name)
            MUL, ADD, SUB, MAX = ALU.mult, ALU.add, ALU.subtract, ALU.max

            v.wait_ge(*after("p_vec"))
            for i in range(2):
                link(v.tensor_copy(vec[0:8, i, 0:VEC], (BC, BY)[i][0:8, 0:VEC]))
            link(v.memset(vec[0:8, :, VEC:VEC + 1], 0.0), "vec")
            v.wait_ge(env["sem"]("params2_in"), 16)
            v.wait_ge(*after("x_rms"))
            link(v.reciprocal(rms, rms))
            for k in range(KD):
                stt(h[:, k, :], x[:, k, :], R("gain", k), rms, MUL, MUL, "h" if k == KD - 1 else None)
            lam = R("lambda", 0, 4)
            stt(sp8[:, 0:4], lam, -1.0, lam, MUL, MAX, name="lam_abs")

            def spread(i, name):
                for g in range(2):
                    for par in range(2):
                        link(v.tensor_copy(kv2[par * HD:(par + 1) * HD, g, 0:T - par],
                                           P0[g * HD:(g + 1) * HD, i * T + par:(i + 1) * T]))
                link_pe = R("pe", 16 * i, 16).unsqueeze(2).broadcast_to([P, 16, NC])
                for g in range(2):
                    tok = bass.AP(kv2.tensor, kv2[:, g, 0:1].offset, [kv2.ap[0], [2, 16], [16, NC]])
                    tt(blk[:, :, g, :], tok, link_pe, ADD, name if g else None)

            v.wait_ge(*after("p_kvc"))
            spread(0, "blk_k")
            for g in range(2):
                for par in range(2):
                    link(v.tensor_copy(kvv[par * HD:(par + 1) * HD, g, 0:T - par],
                                       P0[g * HD:(g + 1) * HD, T + par:2 * T]), "vc_raw" if (g, par) == (1, 1) else None)
            for j in range(2):
                v.wait_ge(*after(f"q{j}_rms"))
                s = tmp[:, 2 * j:2 * j + 2, :]
                link(v.reciprocal(s, s))
                stt(q[:, 2 * j:2 * j + 2, :], q[:, 2 * j:2 * j + 2, :], R("q_gain"), s, MUL, MUL, f"q{j}_n")
            v.wait_ge(*after("k_rms"))
            link(v.reciprocal(mg[:, 0:2, :], mg[:, 0:2, :]))
            for i in range(2):
                stt(kk[:, i, :], kk[:, i, :], R("k_gain", 1 + i), mg[:, i, :], MUL, MUL, "k_n" if i else None)
            v.wait_ge(*after("p_hid_k"))
            for g in range(2):
                tok = bass.AP(kvv.tensor, kvv[:, g, 0:1].offset, [kvv.ap[0], [2, 16], [16, NC]])
                tt(blk[:, :, g, :], tok, R("pe", 16, 16).unsqueeze(2).broadcast_to([P, 16, NC]), ADD, "blk_v" if g else None)
            v.wait_ge(*after("kc_rms"))
            link(v.reciprocal(rms[:, 16:16 + NC], rms[:, 16:16 + NC]))
            stt(kc[:, 0:NC], kc[:, 0:NC], R("k_gain", 0), rms[:, 16:16 + NC], MUL, MUL, "kc")
            v.wait_ge(*after("lam_exp"))
            y, z, z2, acc = (sp8[:, 4 * i:4 * i + 4] for i in range(1, 5))
            ts(acc, y, 2.0, None, ADD)
            link(v.reciprocal(acc, acc))
            tt(z, y, acc, MUL)
            tt(z2, z, z, MUL)
            ts(acc, z2, 1.0 / 17, 1.0 / 15, MUL, ADD)
            for n in (13, 11, 9, 7, 5, 3, 1):
                tt(acc, acc, z2, MUL)
                ts(acc, acc, 1.0 / n, None, ADD)
            tt(acc, acc, z, MUL)
            ts(z, lam, -1.0, 0.0, MUL, MAX)
            stt(acc, acc, 2.0, z, MUL, ADD)
            ts(sp8[:, 36:40], acc, -4.0, None, MUL, name="lam")
            for half in range(2):
                v.wait_ge(*after(f"u{half}"))
                for j in (2 * half, 2 * half + 1):
                    ts(uc[:, j, :], up[:, j, 0:T], R("conv_w", 4 * j), R("conv_b", j), MUL, ADD)
                    for k in range(1, 4):
                        stt(uc[:, j, :], up[:, j, k:k + T], R("conv_w", 4 * j + k), uc[:, j, :], MUL, ADD,
                            f"uc{half}" if (j % 2, k) == (1, 3) else None)
                if half == 0:
                    for b in range(2):
                        v.wait_ge(*after(f"p_cbias_{b}"))
                        link(v.tensor_copy(cbias[:, 8 * b:8 * b + 8, :],
                                           (Z0, Z1)[b][:, 0:8 * NC].rearrange("p (i c) -> p i c", i=8)), f"cbias_{b}")
            for b in range(2):
                v.wait_ge(*after(f"p_csc_{b}"))
                tt(sc[:, 8 * b:8 * b + 8, :], (BY, BX)[b][:, 0:8 * NC].rearrange("p (i c) -> p i c", i=8),
                   cbias[:, 8 * b:8 * b + 8, :], ADD, f"csc_{b}")
            link(v.tensor_reduce(st, sc, AX.X, MAX))
            tt(sc, sc, st.unsqueeze(2).broadcast_to([P, 16, NC]), SUB, "csub")
            v.wait_ge(*after("cexp"))
            link(v.tensor_reduce(st, sc, AX.X, ADD))
            link(v.reciprocal(st, st))
            tt(st2.rearrange("p (h a) -> p a h", a=2), st.rearrange("p (h a) -> p a h", a=2), brg[:, :, 0:8], MUL)
            tt(sc, sc, st2.unsqueeze(2).broadcast_to([P, 16, NC]), MUL)
            for a_ in range(2):
                s = sc.rearrange("p (h a) c -> p a h c", a=2)[:, a_]
                tt(s, s, R("cmp_ok", 16 * a_, NC).unsqueeze(1).broadcast_to([P, 8, NC]), MUL, "cprob" if a_ else None)

            def softmax_in(n):
                v.wait_ge(*after(f"p_scores_{n}"))
                for i, (o0, w) in enumerate(((0, P), (P, T))):
                    c = 2 * n + i
                    link(v.tensor_reduce(mx[:, c:c + 1], (Z0, Z1)[n % 2][:, o0:o0 + w], AX.X, MAX, negate=True),
                         f"shift_{n}" if i else None)

            def softmax_out(n):
                hn, br_ = n // 2, n % 2
                hh = hn // 2 + 4 * (hn % 2)
                pr = prob[n % 2]
                v.wait_ge(*after(f"exp_{n}"))
                c = 2 * n
                link(v.reciprocal(fac[:, c:c + 2], sums[:, c:c + 2]))
                tt(fac[:, c:c + 2], fac[:, c:c + 2], brg[:, :, 8 * (1 + br_) + hh], MUL)
                for i, (o0, w) in enumerate(((0, P), (P, T))):
                    ts(pr[:, o0:o0 + w], pr[:, o0:o0 + w], fac[:, c + i:c + i + 1], None, MUL,
                       name=f"prob_{n}" if i else None)

            for b in range(4):
                v.wait_ge(*after(f"p_pcT_{b}"))
                link(v.tensor_copy(pcT[0:NC, 2 * b:2 * b + 2, :].rearrange("p h t -> p (h t)"), (BC, BO, BY, BX)[b][0:NC, :]),
                     f"pcT_{b}")
            softmax_in(0)
            softmax_in(1)
            v.wait_ge(*after("lru_sqrt"))
            for n in range(16):
                softmax_out(n)
                if n + 2 < 16:
                    softmax_in(n + 2)
                if 1 <= n <= 4:
                    j = n - 1
                    rec = lrec[:, j, :]
                    ts(rec, ru[:, j, :], -1.0, 1.0, MUL, ADD)
                    link(v.reciprocal(rec, rec))
                    stt(ru[:, j, :], ru[:, j, :], 1.0, rec, ADD, MUL)
                    stt(tmp[:, j, :], tmp[:, j, :], 2.0, rec, MUL, MUL)
                    tt(iu[:, j, :], iu[:, j, :], uc[:, j, :], MUL)
                    tt(iu[:, j, :], iu[:, j, :], tmp[:, j, :], MUL)
                    link(v.tensor_tensor_scan(uc[:, j, :], ru[:, j, :], iu[:, j, :], 0.0, MUL, ADD))
                    tt(gl[:, j, :], gl[:, j, :], uc[:, j, :], MUL, "lru" if j == 3 else None)
            for i in range(2):
                v.wait_ge(*after("p_o_15" if i else "p_o_7"))
                tt(o[:, 2 * i:2 * i + 2, :], gn[:, 2 * i:2 * i + 2, :], pair((BO, BX)[i]), MUL, f"o_{i}")
            for name, gate in (("yb", mg), ("ya", mga)):
                for i in range(4):
                    v.wait_ge(*after(f"p_{name}_{i}"))
                    bank = pair((P1, P0)[i % 2])
                    g2 = gate[:, 2 * i:2 * i + 2, :]
                    out = sqx[:, 2 * i:2 * i + 2, :]
                    if name == "yb":
                        stt(out, g2, 1.0, bank, ADD, MUL, f"yb_{i}")
                    else:
                        stt(tmp[:, 0:2, :], g2, 1.0, bank, ADD, MUL, f"ya_{i}")
                        tt(out, out, tmp[:, 0:2, :], ADD, "merged" if i == 3 else None)
            for i in range(4):
                v.wait_ge(*after(f"p_x_{i}"))
                xs = x[:, 2 * i:2 * i + 2, :]
                stt(xs, pair((P1, P0)[i % 2]), 0.5, xs, MUL, ADD, f"x_{i}")
            for a_ in range(TT2):
                for g in range(2):
                    v.wait_ge(*after(f"p_y_{a_}_{g}"))
                    link(v.tensor_copy(ysb[:, a_, g * 512:(g + 1) * 512], (Z0, Z1)[g]), f"yh_{a_}_{g}")


def _colblocks(w):
    n = w.shape[1] // P
    return w.reshape(KD, P, n, P).transpose(2, 1, 0, 3).reshape(n, P, D)


def _rowblocks(w):
    return w.reshape(-1, P, D)


def _chans(a, n):
    return a.reshape(n, P).T


def lay_out(i):
    pad = lambda n: [np.zeros((n, P, D), np.float32)]
    stream = []

    def expert(w1, w3, w2):
        a, b, c = _colblocks(w1), _colblocks(w3), _rowblocks(w2)
        for f in range(FF_TILES):
            stream.extend([a[f:f + 1], b[f:f + 1]])
            if f:
                stream.append(c[f - 1:f])
        stream.append(c[FF_TILES - 1:])

    half = FF_TILES * P
    for l in range(LAYERS):
        stream.append(_colblocks(i["w_in"][l]))
        g, b = i["w_gate"][l], i["w_branch"][l]
        stream += [_colblocks(g[3]), _colblocks(g[2]), _rowblocks(b[3]), _rowblocks(b[2]), _colblocks(g[1]),
                   _colblocks(g[0]), _rowblocks(b[1]), _rowblocks(b[0]), _colblocks(i["w_out"][l])] + pad(3)
        if l == 0:
            for e in range(DENSE_PARTS):
                s = slice(e * half, (e + 1) * half)
                expert(i["ffn_w1"][0][:, s], i["ffn_w3"][0][:, s], i["ffn_w2"][0][s])
        else:
            for e in range(EXPERTS):
                expert(i["moe_w1"][0][e], i["moe_w3"][0][e], i["moe_w2"][0][e])
    w = i["w_in_2"]
    heads = [c for j in range(4) for hh in (j, j + 4) for c in range(hh * HD, (hh + 1) * HD)]
    qb = _colblocks(w[:, 0:512][:, heads])
    kv = _colblocks(w[:, 512:1280])
    gnb = _colblocks(w[:, 1280:1792][:, heads])
    ub, glb = _colblocks(w[:, 1816:2328]), _colblocks(w[:, 2328:2840])
    ga, gb = _colblocks(w[:, 2840:3864]), _colblocks(w[:, 3864:4888])
    cw = i["cmp_w1_2"].reshape(2, 4, 4, P, 256).transpose(0, 1, 3, 2, 4).reshape(2, 4, P, D)
    stream += [kv[0:2], qb, kv[2:3], kv[4:5], kv[3:4], kv[5:6], cw[0], gnb[0:2], cw[1], gnb[2:4], ub, glb, gb, ga,
               _rowblocks(i["w_proj_b_2"]), _rowblocks(i["w_proj_a_2"][heads]), _colblocks(i["w_out_2"])] + pad(4)
    stream = np.concatenate(stream, 0)

    prm = np.zeros((LAYERS, P, PN), np.float32)
    for l in range(LAYERS):
        def put(name, a):
            s, e = PCOL[name]
            prm[l][:, s:e] = a
        put("norm_mix", _chans(i["norm_mix"][l], 8))
        put("norm_ffn", _chans(i["norm_ffn"][l], 8))
        put("mu", _chans(i["rw_mu"][l], 8))
        for name, key in (("w0", "rw_w0"), ("a0", "rw_a0"), ("k_k", "rw_k_k"), ("k_a", "rw_k_a"), ("r_k", "rw_r_k"),
                          ("rw_ln_w", "rw_ln_w"), ("rw_ln_b", "rw_ln_b"), ("ret_gn", "ret_gn"), ("conv_b", "conv_b"),
                          ("conv_ln_w", "conv_ln_w"), ("conv_ln_b", "conv_ln_b")):
            put(name, _chans(i[key][l].reshape(-1), 2))
        put("sb_q", np.tile(i["sb_q_norm"][l], 2)[:, None])
        put("sb_k", np.tile(i["sb_k_norm"][l], 2)[:, None])
        put("dw", i["conv_dw"][l].reshape(TAPS, 2, P).transpose(2, 1, 0).reshape(P, 2 * TAPS))
        put("is_moe", np.full((P, 1), float(l), np.float32))
        put("is_dense", np.full((P, 1), float(1 - l), np.float32))
        put("lora", np.concatenate([np.concatenate([i["rw_w2"][l], i["rw_a2"][l]], 0), i["rw_g2"][l]], 1))
        put("router", i["router"][0].reshape(KD, P, EXPERTS).transpose(1, 0, 2).reshape(P, 64))

    p2 = np.zeros((P, QN), np.float32)

    def put2(name, a):
        s, e = QCOL[name]
        p2[:a.shape[0], s:e] = a
    put2("gain", _chans(i["norm_gain_2"], 8))
    put2("q_gain", np.tile(i["q_norm_gain_2"], 2)[:, None])
    put2("k_gain", np.tile(i["k_norm_gain_2"].T, (2, 1)))
    put2("b1", i["cmp_b1_2"].reshape(4, P).T)
    put2("pe", i["cmp_pe_2"].reshape(2, 16, P).transpose(2, 0, 1).reshape(P, 32))
    put2("w2", i["cmp_w2_2"].reshape(2, 2, P, HD).transpose(2, 0, 1, 3).reshape(P, 256))
    put2("conv_w", i["conv_w_2"].reshape(4, 4, P).transpose(2, 1, 0).reshape(P, 16))
    for name, key in (("conv_b", "conv_b_2"), ("ba", "lru_ba_2"), ("bx", "lru_bx_2"), ("lambda", "lru_lambda_2")):
        put2(name, _chans(i[key], 4))
    for name, key in (("wa", "lru_wa_2"), ("wx", "lru_wx_2")):
        bd = np.zeros((P, 4, P), np.float32)
        for j in range(4):
            bd[0:HD, j, 0:HD] = i[key][2 * j]
            bd[HD:P, j, HD:P] = i[key][2 * j + 1]
        put2(name, bd.reshape(P, 512))
    put2("br", w[:, 1792:1816].reshape(KD, P, 24).transpose(1, 0, 2).reshape(P, 192))
    put2("rel", np.concatenate([i["rel_bias_2"], np.ones((1, HEADS2), np.float32)], 0))
    dist = np.arange(VEC) - (T - 1)
    n = np.maximum(dist, 0)
    large = 16 + (np.log(np.maximum(n, 1).astype(np.float32) / np.float32(16)) / np.float32(np.log(8.0))
                  * np.float32(16)).astype(np.int32)
    bucket = np.where(n < 16, n, np.minimum(large, BUCKETS - 1))
    oh = np.zeros((BUCKETS + 1, VEC), np.float32)
    oh[bucket, np.arange(VEC)] = dist >= 0
    oh[BUCKETS] = np.where(dist >= 0, 0.0, NEG)
    put2("onehot", np.concatenate([oh[:, ::-1], oh], 1))
    t = np.arange(T)[:, None]
    ok = (t - (16 * np.arange(NC)[None, :] + 31) >= 0).astype(np.float32)
    okp = np.zeros((P, 32), np.float32)
    okp[:, 0:NC], okp[:, 16:16 + NC] = ok[0:P], ok[P:T]
    put2("cmp_ok", okp)
    return stream, prm, p2


def kernel(**inputs):
    import concourse.bacc as _bacc
    from concourse.bass_utils import run_bass_kernel_spmd as _run

    i = {k: np.ascontiguousarray(a) for k, a in inputs.items()}
    stream, prm, p2 = lay_out(i)
    arrays = {"x": i["x"], "stream": stream, "params": prm, "params2": p2, "consts": constants()}

    def build(known):
        nc = _bacc.Bacc("TRN2", target_bir_lowering=False, num_devices=1)
        dram = {n: nc.dram_tensor(n, a.shape, F32, kind="ExternalInput").ap() for n, a in arrays.items()}
        dram["out"] = nc.dram_tensor("out", (1, T, D), F32, kind="ExternalOutput").ap()
        dram["bias_vec"] = nc.dram_tensor("bias_vec", (16, 512), F32, kind="Internal").ap()
        return nc, program(nc, dram, known)

    _, steps = build(None)
    nc, _ = build(steps)
    return _run(nc, [arrays], core_ids=[0]).results[0]["out"]
```
